# Optimizing a Trainium2 kernel written in Bass

```python
import jax, jax.numpy as jnp
from jax import lax
import numpy as np

D_MODEL = 1024
BATCH = 1
SEQ = 512
DEPTH = 1
DEC_BATCH = 8
DEC_SEQ = 8
PAST_LEN = 4096
PAGE_SIZE = 128

N_META = 16
SSD_INNER = 2 * D_MODEL
SSD_HEAD_DIM = 64
SSD_HEADS = SSD_INNER // SSD_HEAD_DIM
SSD_GROUPS = 4
SSD_HPG = SSD_HEADS // SSD_GROUPS
SSD_STATE = 128
SSD_CONV = 4
SSD_CONV_DIM = SSD_INNER + 2 * SSD_GROUPS * SSD_STATE
SSD_CHUNK = 128
SC_WIDTH = D_MODEL
SC_CONV = 3
N_EGROUPS = 4
EXPERTS_PER_GROUP = 8
N_EXPERTS = N_EGROUPS * EXPERTS_PER_GROUP
TOP_K = 2
D_EXPERT = D_MODEL // 4
EPS = 1e-6
COL_SIZES = (SSD_INNER, SSD_CONV_DIM, SSD_HEADS, SC_WIDTH, SC_WIDTH, SC_WIDTH, D_MODEL, D_MODEL)
IN_COLS = sum(COL_SIZES)

kernel_name = 'hybrid_ssd_shortconv_hiermoe_step'

def _rmsnorm(x, w):
    xf = x.astype(jnp.float32)
    xf = xf * lax.rsqrt(jnp.mean(xf * xf, axis=-1, keepdims=True) + EPS)
    return (xf * w.astype(jnp.float32)).astype(x.dtype)

def _causal_dwconv(u, hist, w):
    K = w.shape[0]
    L = u.shape[1]
    full = jnp.concatenate([hist.astype(u.dtype), u], axis=1)
    out = full[:, 0:L] * w[0]
    for k in range(1, K):
        out = out + full[:, k:k + L] * w[k]
    return out, full[:, L:]

def _ssd_chunked(x, dt, a_neg, Bm, Cm, h0, chunk):
    f32 = jnp.float32
    b, L = x.shape[0], x.shape[1]
    nc = L // chunk
    G, R, P, N = SSD_GROUPS, SSD_HPG, SSD_HEAD_DIM, SSD_STATE
    x = x.astype(f32).reshape(b, nc, chunk, G, R, P)
    dt = dt.astype(f32).reshape(b, nc, chunk, G, R)
    Bm = Bm.astype(f32).reshape(b, nc, chunk, G, N)
    Cm = Cm.astype(f32).reshape(b, nc, chunk, G, N)
    acum = jnp.cumsum(dt * a_neg.reshape(G, R), axis=2)
    causal = jnp.tril(jnp.ones((chunk, chunk), dtype=bool))
    seg = acum[:, :, :, None] - acum[:, :, None, :]
    decay = jnp.exp(jnp.where(causal[:, :, None, None], seg, -jnp.inf))
    cb = jnp.einsum('bclgn,bcsgn->bclsg', Cm, Bm)
    wts = cb[..., None] * decay * dt[:, :, None]
    y_diag = jnp.einsum('bclsgr,bcsgrp->bclgrp', wts, x)
    to_end = jnp.exp(acum[:, :, -1:] - acum) * dt
    states = jnp.einsum('bclgn,bclgr,bclgrp->bcgrpn', Bm, to_end, x)
    chunk_decay = jnp.exp(acum[:, :, -1])

    def step(h, inp):
        s_c, d_c = inp
        return d_c[..., None, None] * h + s_c, h

    h_last, h_prev = lax.scan(step, h0.astype(f32).reshape(b, G, R, P, N),
                              (jnp.moveaxis(states, 1, 0), jnp.moveaxis(chunk_decay, 1, 0)))
    h_prev = jnp.moveaxis(h_prev, 0, 1)
    y_off = jnp.einsum('bclgn,bcgrpn,bclgr->bclgrp', Cm, h_prev, jnp.exp(acum))
    y = (y_diag + y_off).reshape(b, L, SSD_HEADS, P)
    return y, h_last.reshape(b, SSD_HEADS, P, N)

def _token_mixers(h, ssm0, conv_hist, sc_hist, segments, w_in, conv_w, conv_b, dt_bias, A_log,
                  D_skip, norm_w, w_ssd_out, sc_conv_w, w_sc_out, w_o):
    f32 = jnp.float32
    b, L, _ = h.shape
    idx = [int(i) for i in np.cumsum(COL_SIZES)[:-1]]
    z, xbc, dt_raw, sc_b, sc_c, sc_h, g_ssd, g_sc = jnp.split(h @ w_in, idx, axis=-1)
    xbc, conv_hist_new = _causal_dwconv(xbc, conv_hist, conv_w)
    xbc = jax.nn.silu(xbc + conv_b)
    xs, Bm, Cm = jnp.split(xbc, [SSD_INNER, SSD_INNER + SSD_GROUPS * SSD_STATE], axis=-1)
    xs = xs.reshape(b, L, SSD_HEADS, SSD_HEAD_DIM)
    Bm = Bm.reshape(b, L, SSD_GROUPS, SSD_STATE)
    Cm = Cm.reshape(b, L, SSD_GROUPS, SSD_STATE)
    dt = jax.nn.softplus((dt_raw + dt_bias).astype(f32))
    a_neg = -jnp.exp(A_log.astype(f32))
    hstate = ssm0
    ys = []
    start = 0
    for length, chunk in segments:
        sl = slice(start, start + length)
        y_seg, hstate = _ssd_chunked(xs[:, sl], dt[:, sl], a_neg, Bm[:, sl], Cm[:, sl], hstate, chunk)
        ys.append(y_seg)
        start += length
    y = jnp.concatenate(ys, axis=1) + xs.astype(f32) * D_skip.astype(f32)[:, None]
    u = y.reshape(b, L, SSD_INNER) * jax.nn.silu(z.astype(f32))
    ug = u.reshape(b, L, SSD_GROUPS, SSD_INNER // SSD_GROUPS)
    ug = ug * lax.rsqrt(jnp.mean(ug * ug, axis=-1, keepdims=True) + EPS)
    u = (ug.reshape(b, L, SSD_INNER) * norm_w.astype(f32)).astype(h.dtype)
    y_ssd = u @ w_ssd_out
    cout, sc_hist_new = _causal_dwconv(sc_c * sc_h, sc_hist, sc_conv_w)
    y_sc = (sc_b * cout) @ w_sc_out
    merged = jax.nn.sigmoid(g_ssd) * y_ssd + jax.nn.sigmoid(g_sc) * y_sc
    return merged @ w_o, hstate.astype(h.dtype), conv_hist_new, sc_hist_new

def _hier_moe(h, w_rg, b_rg, w_re, b_re, w_gate, w_up, w_down):
    f32 = jnp.float32
    shp = h.shape
    t = h.reshape(-1, D_MODEL)
    p_grp = jax.nn.softmax((t @ w_rg + b_rg).astype(f32), axis=-1)
    g_sel = jnp.argmax(p_grp, axis=-1)
    g_prob = jnp.take_along_axis(p_grp, g_sel[:, None], axis=-1)
    le = (t @ w_re + b_re).astype(f32).reshape(-1, N_EGROUPS, EXPERTS_PER_GROUP)
    le = jnp.take_along_axis(le, g_sel[:, None, None], axis=1)[:, 0]
    p_exp = jax.nn.softmax(le, axis=-1)
    top_v, top_i = lax.top_k(p_exp, TOP_K)
    top_v = top_v / jnp.sum(top_v, axis=-1, keepdims=True)
    w_local = jnp.einsum('tk,tke->te', top_v, jax.nn.one_hot(top_i, EXPERTS_PER_GROUP, dtype=f32)) * g_prob
    gate = (jax.nn.one_hot(g_sel, N_EGROUPS, dtype=f32)[:, :, None] * w_local[:, None, :]).astype(h.dtype)
    out = jnp.zeros_like(t)
    for g in range(N_EGROUPS):
        a = jnp.einsum('td,edf->tef', t, w_gate[g])
        up = jnp.einsum('td,edf->tef', t, w_up[g])
        act = jax.nn.silu(a) * up * gate[:, g, :, None]
        out = out + jnp.einsum('tef,efd->td', act, w_down[g])
    return out.reshape(shp)

def setup_inputs(seed: int = 0) -> dict:
    key = jax.random.key(seed)
    ks = jax.random.split(key, 32)
    nrm = jax.random.normal
    f32 = jnp.float32
    dt0 = jnp.exp(jax.random.uniform(ks[10], (DEPTH, SSD_HEADS), f32) * (np.log(0.1) - np.log(0.001)) + np.log(0.001))
    dt_bias = dt0 + jnp.log(-jnp.expm1(-dt0))
    return {
        'x_prompt': nrm(ks[0], (BATCH, SEQ, D_MODEL), f32),
        'x_sample': nrm(ks[1], (DEC_BATCH, DEC_SEQ, D_MODEL), f32),
        'state_ssm': 0.1 * nrm(ks[2], (DEPTH, DEC_BATCH, SSD_HEADS, SSD_HEAD_DIM, SSD_STATE), f32),
        'state_ssd_conv': nrm(ks[3], (DEPTH, DEC_BATCH, SSD_CONV - 1, SSD_CONV_DIM), f32),
        'state_short_conv': nrm(ks[4], (DEPTH, DEC_BATCH, SC_CONV - 1, SC_WIDTH), f32),
        'meta_tokens': nrm(ks[5], (N_META, D_MODEL), f32),
        'ln1_w': 1.0 + 0.02 * nrm(ks[6], (DEPTH, D_MODEL), f32),
        'w_in': nrm(ks[7], (DEPTH, D_MODEL, IN_COLS), f32) * D_MODEL ** -0.5,
        'ssd_conv_w': nrm(ks[8], (DEPTH, SSD_CONV, SSD_CONV_DIM), f32) * SSD_CONV ** -0.5,
        'ssd_conv_b': 0.01 * nrm(ks[9], (DEPTH, SSD_CONV_DIM), f32),
        'ssd_dt_bias': dt_bias,
        'ssd_A_log': jnp.log(jax.random.uniform(ks[11], (DEPTH, SSD_HEADS), f32, 1.0, 16.0)),
        'ssd_D': 1.0 + 0.1 * nrm(ks[12], (DEPTH, SSD_HEADS), f32),
        'ssd_norm_w': 1.0 + 0.02 * nrm(ks[13], (DEPTH, SSD_INNER), f32),
        'w_ssd_out': nrm(ks[14], (DEPTH, SSD_INNER, D_MODEL), f32) * SSD_INNER ** -0.5,
        'sc_conv_w': nrm(ks[15], (DEPTH, SC_CONV, SC_WIDTH), f32) * SC_CONV ** -0.5,
        'w_sc_out': nrm(ks[16], (DEPTH, SC_WIDTH, D_MODEL), f32) * SC_WIDTH ** -0.5,
        'w_o': nrm(ks[17], (DEPTH, D_MODEL, D_MODEL), f32) * D_MODEL ** -0.5,
        'ln2_w': 1.0 + 0.02 * nrm(ks[18], (DEPTH, D_MODEL), f32),
        'w_rg': nrm(ks[19], (DEPTH, D_MODEL, N_EGROUPS), f32) * D_MODEL ** -0.5,
        'b_rg': 0.01 * nrm(ks[20], (DEPTH, N_EGROUPS), f32),
        'w_re': nrm(ks[21], (DEPTH, D_MODEL, N_EXPERTS), f32) * D_MODEL ** -0.5,
        'b_re': 0.01 * nrm(ks[22], (DEPTH, N_EXPERTS), f32),
        'w_gate': nrm(ks[23], (DEPTH, N_EGROUPS, EXPERTS_PER_GROUP, D_MODEL, D_EXPERT), f32) * D_MODEL ** -0.5,
        'w_up': nrm(ks[24], (DEPTH, N_EGROUPS, EXPERTS_PER_GROUP, D_MODEL, D_EXPERT), f32) * D_MODEL ** -0.5,
        'w_down': nrm(ks[25], (DEPTH, N_EGROUPS, EXPERTS_PER_GROUP, D_EXPERT, D_MODEL), f32) * D_EXPERT ** -0.5,
        'final_norm_w': 1.0 + 0.02 * nrm(ks[26], (D_MODEL,), f32),
    }

def reference(x_prompt, x_sample, state_ssm, state_ssd_conv, state_short_conv, meta_tokens, ln1_w, w_in,
              ssd_conv_w, ssd_conv_b, ssd_dt_bias, ssd_A_log, ssd_D, ssd_norm_w, w_ssd_out, sc_conv_w,
              w_sc_out, w_o, ln2_w, w_rg, b_rg, w_re, b_re, w_gate, w_up, w_down, final_norm_w):
    dtype = x_prompt.dtype
    bp, sp = x_prompt.shape[0], x_prompt.shape[1]
    bs, ss = x_sample.shape[0], x_sample.shape[1]
    xp = jnp.concatenate([jnp.broadcast_to(meta_tokens.astype(dtype)[None], (bp, N_META, D_MODEL)), x_prompt], axis=1)
    xs = x_sample
    seg_prompt = ((N_META, N_META), (sp, SSD_CHUNK))
    seg_sample = ((ss, ss),)
    ssm_p, cv_p, sc_p, ssm_s, cv_s, sc_s = [], [], [], [], [], []
    for l in range(DEPTH):
        mix_w = (w_in[l], ssd_conv_w[l], ssd_conv_b[l], ssd_dt_bias[l], ssd_A_log[l], ssd_D[l],
                 ssd_norm_w[l], w_ssd_out[l], sc_conv_w[l], w_sc_out[l], w_o[l])
        moe_w = (w_rg[l], b_rg[l], w_re[l], b_re[l], w_gate[l], w_up[l], w_down[l])
        m, h1, c1, s1 = _token_mixers(_rmsnorm(xp, ln1_w[l]),
                                      jnp.zeros((bp, SSD_HEADS, SSD_HEAD_DIM, SSD_STATE), jnp.float32),
                                      jnp.zeros((bp, SSD_CONV - 1, SSD_CONV_DIM), dtype),
                                      jnp.zeros((bp, SC_CONV - 1, SC_WIDTH), dtype),
                                      seg_prompt, *mix_w)
        xp = xp + m
        xp = xp + _hier_moe(_rmsnorm(xp, ln2_w[l]), *moe_w)
        ssm_p.append(h1)
        cv_p.append(c1)
        sc_p.append(s1)
        m, h2, c2, s2 = _token_mixers(_rmsnorm(xs, ln1_w[l]), state_ssm[l], state_ssd_conv[l],
                                      state_short_conv[l], seg_sample, *mix_w)
        xs = xs + m
        xs = xs + _hier_moe(_rmsnorm(xs, ln2_w[l]), *moe_w)
        ssm_s.append(h2)
        cv_s.append(c2)
        sc_s.append(s2)
    y_prompt = _rmsnorm(xp, final_norm_w)[:, N_META:]
    y_sample = _rmsnorm(xs, final_norm_w)
    return (y_prompt, y_sample, jnp.stack(ssm_p, 0), jnp.stack(cv_p, 0), jnp.stack(sc_p, 0),
            jnp.stack(ssm_s, 0), jnp.stack(cv_s, 0), jnp.stack(sc_s, 0))


_drawn_inputs = setup_inputs


def setup_inputs(seed=0):
    import zlib

    import numpy as np

    out = dict(_drawn_inputs(seed))
    spreads = {}
    factors = {'ssd_conv_b': 2.941,
     'ssd_norm_w': 2.821,
     'b_rg': 15.456,
     'b_re': 4.891,
     'final_norm_w': 7.827,
     'ln2_w': 3.053}
    for name, (base, spread) in spreads.items():
        noise = np.random.default_rng([zlib.crc32(name.encode()), seed]).standard_normal(out[name].shape)
        drawn = base * np.exp(spread * noise) if base else spread * noise
        out[name] = __import__('jax').numpy.asarray(drawn.astype(out[name].dtype))
    for name, factor in factors.items():
        out[name] = (out[name] * factor).astype(out[name].dtype)
    return out
```

```python
import concourse.bass as bass
from concourse import mybir
from contextlib import ExitStack

F32 = mybir.dt.float32
F32R = mybir.dt.float32r
I32 = mybir.dt.int32
ALU = mybir.AluOpType
ACT = mybir.ActivationFunctionType
AX = mybir.AxisListType

P = 128
D = 1024
DEPTH_K = D // P
N_META, SEQ = 16, 512
TP = N_META + SEQ
NSEQ, SLEN = 8, 8
TS = NSEQ * SLEN
T = TP + TS
TILES = 5
ROWS = [P] * 4 + [T - 4 * P]
LASTP = TP - 4 * P
HALF = TP // 2
HEADS, HD, NST, GROUPS = 32, 64, 128, 4
HPG = HEADS // GROUPS
INNER = HEADS * HD
GW = INNER // GROUPS
GK = GW // P
CONV = INNER + 2 * GROUPS * NST
XT_TILES = CONV // P
COL_Z, COL_X = 0, INNER
COL_DT = COL_X + CONV
COL_SB = COL_DT + HEADS
COL_SC, COL_SH = COL_SB + D, COL_SB + 2 * D
COL_GSSD, COL_GSC = COL_SB + 3 * D, COL_SB + 4 * D
XH, SH = 3, 2
XROW, SROW = XH + SLEN, SH + SLEN
XPAD, SPAD = XH + TP + NSEQ * XROW, SH + TP + NSEQ * SROW
XCONV, SCONV = XPAD - XH, SPAD - SH
NEG, NE, EPG, FE = 4, 32, 8, 256
FK = FE // P
CAP = 96
ROUNDS = -(-(T - CAP) // CAP)
SLOTS = CAP * (1 + ROUNDS)
EPS = 1e-6
TAIL = XH * (1 + NSEQ)
STAIL = SH * (1 + NSEQ)
BLK = 8 * P
UNROLL = 4


def tok(i):
    return slice(i * P, i * P + ROWS[i])


def build(nc, ins, outs):
    ctx = ExitStack()
    with ctx:
        def sem(name):
            return ctx.enter_context(nc.semaphore(name))

        def sb(name, shape, dt=F32):
            return ctx.enter_context(nc.sbuf_tensor(name, shape, dt))[tuple(slice(None) for _ in shape)]

        def bank(name, shape):
            return ctx.enter_context(nc.psum_tensor(name, shape, F32))[tuple(slice(None) for _ in shape)]

        ident = sb("ident", [P, P])
        m_le = sb("m_le", [P, P])
        m_gt = sb("m_gt", [P, P])
        ones = sb("ones", [P, P])
        R4 = ROWS[4]
        m_le4 = sb("m_le4", [R4, R4])
        m_gt4 = sb("m_gt4", [R4, R4])
        m_blk4 = sb("m_blk4", [R4, R4])
        eps = sb("eps", [P, 1])
        stat = sb("stat", [P, 4, TILES])
        svec = sb("svec", [P, 8, 20])
        dnv = sb("dnv", [P, 16, 2])
        xvec = sb("xvec", [P, XT_TILES, 29])
        xtail = sb("xtail", [P, XT_TILES, TAIL])
        stail = sb("stail", [P, 8, STAIL])
        dt_, da = sb("dt", [P, TILES, HEADS]), sb("da", [P, TILES, HEADS])
        e_acum, dte, dec = (sb(n, [P, TILES, HEADS]) for n in ("e_acum", "dte", "dec"))
        sdec = sb("sdec", [R4, HEADS])
        dg = sb("dg", [P, GK, 2])
        BIG, RING, AREA = 40 * T, 6 * BLK, 19852
        with (nc.sbuf_tensor("big", [P, BIG], F32) as big, nc.sbuf_tensor("ring", [P, RING], F32) as ring,
              nc.sbuf_tensor("area", [P, AREA], F32) as area):
            big, ring, area = big[:, :], ring[:, :], area[:, :]
        h_parts, _, u_parts = sb("h_parts", [P, 16 * T], F32R), sb("merged_place", [P, 8 * T]), sb("u_parts", [P, 16 * T], F32R)
        ring_parts, area_parts = sb("ring_parts", [P, RING], F32R), sb("area_parts", [P, AREA], F32R)

        def rows_at(where, at, k):
            return where[:, at:at + k * T].rearrange("p (k t) -> p k t", k=k)

        hT_hi, hT_lo = rows_at(h_parts, 0, 8), rows_at(h_parts, 8 * T, 8)
        mT = rows_at(big, 16 * T, 8)
        hT = mT
        sco_hi, sco_lo = rows_at(u_parts, 0, 8), rows_at(u_parts, 8 * T, 8)
        uT, uT_hi = rows_at(big, 24 * T, 16), rows_at(area_parts, 2048, 16)
        uT_lo = rows_at(u_parts, 0, 16)

        def carve(at, shape, area=area, size=AREA):
            n = 1
            for s in shape:
                n *= s
            v = area[:, at:at + n]
            assert at + n <= size, (at, n)
            if len(shape) == 2:
                v = v.rearrange("p (a b) -> p a b", a=shape[0])
            if len(shape) == 3:
                v = v.rearrange("p (a b c) -> p a b c", a=shape[0], b=shape[1])
            return v, at + n

        w_raw = [ring[:, BLK * s:BLK * (s + 1)].rearrange("p (k f) -> p k f", k=8) for s in range(2)]
        w_hi, w_lo = ([ring_parts[:, BLK * s:BLK * (s + 1)].rearrange("p (k f) -> p k f", k=8) for s in (a, a + 1)]
                      for a in (2, 4))
        x_tok, o = carve(0, [TILES, D])
        h_tok, o = carve(o, [2, D])
        junk, o = carve(o, [D])
        v3, o = carve(o, [CONV])
        v1, o = carve(o, [D])
        v2, o = carve(o, [INNER])
        drow, o = carve(o, [HEADS])
        wdt, o = carve(o, [8, HEADS])
        dtb, o = carve(o, [HEADS])
        ea, o = carve(o, [HEADS])
        dtw, o = carve(o, [6, TILES * HEADS])
        s_c, so = carve(0, [2, T])
        s_o, so = carve(so, [2, T])
        s_pad, so = carve(o, [2, SPAD])
        s_cv, so = carve(so, [2, SPAD])
        xdt, o = carve(0, [2, GW])
        xte, o = carve(o, [2, GW])
        xT, o = carve(o, [GK, T])
        bT, o = carve(o, [T])
        cT, o = carve(o, [T])
        sz, o = carve(o, [GK, T])
        raw, o = carve(o, [2, XPAD])
        cv, o = carve(o, [2, XPAD])
        rbuf, o = carve(o, [2, 4 * P])
        bmask, _ = carve(o - 8 * P, [NSEQ, NST])
        wts, o = carve(o, [2, 4 * P])
        rms, _ = carve(o, [T])
        ytok, o = carve(o, [GW])
        cbm, o = carve(o, [P])
        hs, o = carve(o, [GK, NSEQ, NST])
        h0T, o = carve(o, [2, GW])
        st, o = carve(o, [GW])
        cmask, o = carve(o, [10 * R4])
        btok, o = carve(o, [2, NST])
        df, o = carve(o, [GK, NSEQ])
        dx = xdt[:, 1, :]
        sq = xT
        sg, _ = carve(0, [3, T])
        WE = 3 * 2048
        tails, _ = carve(16 * T, [CONV + D], big, BIG)
        B5 = BIG
        x2, b = carve(0, [TILES, D], big, B5)
        ln2b, b = carve(b, [D], big, B5)
        fnb, b = carve(b, [D], big, B5)
        h2, b = carve(b, [2, D], big, B5)
        wo = [carve(2048 + 16 * T, [8, 512])[0], carve(24 * T, [8, 512], big, B5)[0]]
        h2T, b = carve(24 * T + 4096, [2, 8, P], big, B5)
        router_w, b = carve(b, [8, NEG + NE], big, B5)
        router_b, b = carve(b, [NEG + NE], big, B5)
        before, b = carve(b, [TILES - 1, NE], big, B5)
        m_lt, b = carve(b, [P], big, B5)
        lg, b = carve(b, [TILES, NEG + NE], big, B5)
        pr, b = carve(b, [TILES, NEG, EPG], big, B5)
        m1, b = carve(b, [TILES, NEG, EPG], big, B5)
        m2, b = carve(b, [TILES, NEG, EPG], big, B5)
        mm, b = carve(b, [TILES, NE], big, B5)
        ohg, b = carve(b, [TILES, NEG], big, B5)
        t4, b = carve(b, [TILES, NEG], big, B5)
        le_, b = carve(b, [TILES, EPG], big, B5)
        oh1, b = carve(b, [TILES, EPG], big, B5)
        oh2, b = carve(b, [TILES, EPG], big, B5)
        t8, b = carve(b, [TILES, EPG], big, B5)
        sc, b = carve(b, [13, TILES], big, B5)
        ramp, b = carve(b, [NEG + EPG], big, B5)
        eoff, b = carve(b, [NE], big, B5)
        tokid, b = carve(b, [TILES], big, B5)
        places, b = carve(b, [CAP], big, B5)
        at_slot, o = carve(3 * WE, [2 * TILES, CAP])
        tok_of, o = carve(o, [2 * TILES, NE])
        zero, b = carve(b, [NE * SLOTS // P], big, B5)
        sqj = carve(b, [D], big, B5)[0]
        slot_of, first_of_, later_of = ([sb(f"{n}{k}", [P, TILES], I32) for k in range(2)] for n in ("slot_of", "first_of", "later_of"))
        gate, gate_later = sb("gate", [P, 2, TILES]), sb("gate_later", [P, 2, TILES])
        ids = sb("ids", [CAP, NE + 1], I32)
        idx = [sb(f"idx{u}", [CAP, 1], I32) for u in range(UNROLL)]
        most = sb("most", [1, 1], I32)
        idf = sb("idf", [CAP, 1])
        xe = [carve(24 * T + D * u, [D], big, B5)[0] for u in range(UNROLL)]
        y_in = [carve(D * n, [D])[0] for n in range(2 * TILES)]
        xeT = [carve(24 * T + 4096 + 8 * CAP * u, [8, CAP], big, B5)[0] for u in range(2)]
        gs = [carve(24 * T + 4096 + 16 * CAP + FK * CAP * u, [FK, CAP], big, B5)[0] for u in range(2)]
        ye = [h2[:, u, :] for u in range(2)]

        def expert_slot(u):
            v = ring[:, 0:WE] if u == 3 else area[:, u * WE:(u + 1) * WE]
            return (v[:, 0:2048].rearrange("p (k f) -> p k f", k=8), v[:, 2048:4096].rearrange("p (k f) -> p k f", k=8),
                    v[:, 4096:6144].rearrange("p (k f) -> p k f", k=FK))

        wexp = [expert_slot(u) for u in range(UNROLL)]
        h2_rows = nc.dram_tensor("h2_rows", [T, D], F32).ap()
        id_tab = nc.dram_tensor("id_tab", [NE * SLOTS, 1], F32).ap()
        y_first = nc.dram_tensor("y_first", [NE * CAP, D], F32).ap()
        y_later = nc.dram_tensor("y_later", [NE * ROUNDS * CAP, D], F32).ap()

        acc = [bank(f"acc{i}", [P, 2, 512]) for i in range(2)]
        pT, pS, pY, pO = (bank(n, [P, 512]) for n in ("pT", "pS", "pY", "pO"))

        x_in = [sem(f"x_in{i}") for i in range(TILES)]
        v1_in, vec_in = sem("v1_in"), sem("vec_in")
        consts = sem("consts")
        pool_chain, dve_chain, act_chain = sem("pool_chain"), sem("dve_chain"), sem("act_chain")
        s_sd, s_dexp, s_vtr, s_vcp, s_htok, s_htr, s_hT = (
            sem(n) for n in ("s_sd", "s_dexp", "s_vtr", "s_vcp", "s_htok", "s_htr", "s_hT"))
        s_dtmm, s_dtv, s_dta, s_cum = (sem(n) for n in ("s_dtmm", "s_dtv", "s_dta", "s_cum"))
        raw_in = [sem(f"raw_in{s}") for s in range(2)]
        hi_done = sem("hi_done")
        lo_done = sem("lo_done")
        w_done = sem("w_done")
        h_hi, h_lo, s_sco, s_sz, u_hi, u_lo = (sem(n) for n in ("h_hi", "h_lo", "s_sco", "s_sz", "u_hi", "u_lo"))
        acc_free = [sem(f"acc_free{s}") for s in range(2)]
        c_hist, c_conv, c_tail = (sem(n) for n in ("c_hist", "c_conv", "c_tail"))
        s_hist, s_tail, s_cvd, s_silu = (sem(n) for n in ("s_hist", "s_tail", "s_cvd", "s_silu"))
        p_xt, p_cb, p_seg, p_yo, p_y, p_sn, p_yt = (sem(n) for n in ("p_xt", "p_cb", "p_seg", "p_yo", "p_y", "p_sn", "p_yt"))
        s_u, s_y1, s_y2, s_xd, s_cb, s_bt, s_r, s_exp, s_w, s_st = (
            sem(n) for n in ("s_u", "s_y1", "s_y2", "s_xd", "s_cb", "s_bt", "s_r", "s_exp", "s_w", "s_st"))
        s_dx, p_df, s_df, s_cm, s_bm, hs_in, hs_out, p_h0, s_h0, p_yb, p_hs, s_hd, s_hs = (
            sem(n) for n in ("s_dx", "p_df", "s_df", "s_cm", "s_bm", "hs_in", "hs_out", "p_h0", "s_h0", "p_yb", "p_hs", "s_hd", "s_hs"))
        p_so, so_out, s_uz, s_sq, p_gn, s_rm, s_so = (
            sem(n) for n in ("p_so", "so_out", "s_uz", "s_sq", "p_gn", "s_rm", "s_so"))
        p_tl, s_tl, tails_out = sem("p_tl"), sem("s_tl"), sem("tails_out")
        s_un = sem("s_un")
        o_sg, o_m = sem("o_sg"), sem("o_m")
        wo_in, x_again, row_in, h2_out, id_zero = (
            [sem("wo_in0"), sem("wo_in1")], sem("x_again"), sem("row_in"), [sem("h2_out0"), sem("h2_out1")], sem("id_zero"))
        r_mm, r_x2, r_sd, r_h2, r_tr, r_h2T, r_lg, r_dve, r_act, r_hot, r_pos, r_slot, r_tab, r_sel, r_idtr, r_ids, r_const = (
            sem(n) for n in ("r_mm", "r_x2", "r_sd", "r_h2", "r_tr", "r_h2T", "r_lg", "r_dve", "r_act", "r_hot", "r_pos",
                             "r_slot", "r_tab", "r_sel", "r_idtr", "r_ids", "r_const"))
        e_in = [sem(f"e_in{u}") for u in range(UNROLL)]
        e_done = [sem(f"e_done{u}") for u in range(UNROLL)]
        xe_in = [sem(f"xe_in{u}") for u in range(UNROLL)]
        ye_out = [sem(f"ye_out{u}") for u in range(2)]
        m_idx, m_tr, m_xe, m_gu, m_silu, m_act, m_dn, m_ye = (
            sem(n) for n in ("m_idx", "m_tr", "m_xe", "m_gu", "m_silu", "m_act", "m_dn", "m_ye"))
        f_back, f_add = sem("f_back"), sem("f_add")
        f_w, f_id, f_cast, f_x, f_tr, f_xe, f_gu, f_silu, f_act, f_dn, f_ye, f_out, f_skip = (
            sem(n) for n in ("f_w", "f_id", "f_cast", "f_x", "f_tr", "f_xe", "f_gu", "f_silu", "f_act", "f_dn", "f_ye",
                             "f_out", "f_skip"))
        g_in = [sem(f"g_in{i}") for i in range(TILES)]
        z_ss, z_sd, z_y, y_out = (sem(n) for n in ("z_ss", "z_sd", "z_y", "y_out"))

        def s_block(turn, b):
            return turn * 6 + b, turn * 3 + b // 2, b % 2, turn * 3 + b // 2

        def o1_block(f, b):
            return f * 2 + (24 + b), f + 12, b % 2, f + 12

        def g_block(turn, b):
            return turn * 10 + (40 + b), turn * 5 + (20 + b // 2), b % 2, turn * 5 + (20 + b // 2)

        def o2_block(turn, b):
            q = (0, 1, 2, 2, 3, 3, 4)[b]
            return turn * 6 + (80 + b), turn * 3 + (40 + b // 2), q % 2, turn * 2 + (40 + q // 2)

        BLOCKS = 104

        held = {}

        def hold(eng, s, value):
            eng.wait_ge(s, value)
            eng.sem_inc(held[id(eng)], 1)

        def conv_tile(turn, c):
            return turn + (20 if c == 0 else 16) if c < 2 else turn * GK + (c - 2)

        def chain(eng, s, start, turn=0, per_turn=0):
            k = [0]

            def link(instr):
                k[0] += 1
                instr.then_inc(s, 1)
                eng.wait_ge(s, turn * per_turn + (start + k[0]))
                if per_turn:
                    assert k[0] <= per_turn, "per_turn"
            link.count = k
            return link

        def halves(v):
            return v[:, 0:TP].rearrange("p (a b) -> p a b", a=2), v[:, TP:T]

        def pad_parts(v, hist, row):
            a = v[:, hist:hist + TP].rearrange("p (a b) -> p a b", a=2)
            b = v[:, hist + TP:hist + TP + NSEQ * row].rearrange("p (s c) -> p s c", c=row)
            return a, b[:, :, hist:row]

        def conv_parts(v, hist, row):
            a = v[:, 0:TP].rearrange("p (a b) -> p a b", a=2)
            b = v[:, hist + TP:hist + TP + NSEQ * row].rearrange("p (s c) -> p s c", c=row)
            return a, b[:, :, 0:SLEN]

        def acc_parts(a):
            return a[:, :, 0:HALF], a[:, 1, HALF:HALF + TS]

        seqs = "p (s c) -> p s c"
        def cols(w, at, n):
            c = slice(at, at + n) if isinstance(at, int) else bass.ds(at, n)
            return w[:, c].rearrange("(k p) f -> p k f", p=P)

        def w_in_cols(at, n):
            return cols(ins["w_in"][0], at, n)

        block = ctx.enter_context(nc.Block())

        @block.sync
        def _(sp):
            held[id(sp)] = sem("held_sp")
            xp, xs, meta = ins["x_prompt"][0], ins["x_sample"].rearrange("b s d -> (b s) d"), ins["meta_tokens"]
            sp.dma_start(x_tok[0:N_META, 0, :], meta).then_inc(x_in[0], 16)
            sp.dma_start(x_tok[N_META:P, 0, :], xp[0:P - N_META, :]).then_inc(x_in[0], 16)
            sp.dma_start(v1[0:3, :], ins["sc_conv_w"][0]).then_inc(v1_in, 16)
            sp.dma_start(v1[3:19, :], ins["state_short_conv"][0].rearrange("b r c -> (b r) c")).then_inc(v1_in, 16)
            sp.dma_start(v1[19:20, :], ins["ln1_w"]).then_inc(v1_in, 16)
            sp.dma_start(v3[0:4, :], ins["ssd_conv_w"][0]).then_inc(vec_in, 16)
            sp.dma_start(v3[4:5, :], ins["ssd_conv_b"]).then_inc(vec_in, 16)
            sp.dma_start(v3[5:29, :], ins["state_ssd_conv"][0].rearrange("b r c -> (b r) c")).then_inc(vec_in, 16)
            sp.dma_start(v2[1:2, :], ins["ssd_norm_w"]).then_inc(vec_in, 16)
            sp.dma_start(drow[0:1, :], ins["ssd_D"]).then_inc(vec_in, 16)
            sp.dma_start(dtb, ins["ssd_dt_bias"].broadcast_to([P, HEADS])).then_inc(vec_in, 16)
            sp.dma_start(ea, ins["ssd_A_log"].broadcast_to([P, HEADS])).then_inc(vec_in, 16)
            sp.dma_start(wdt, w_in_cols(COL_DT, HEADS)).then_inc(vec_in, 16)
            for i in range(1, 4):
                r0 = i * P - N_META
                sp.dma_start(x_tok[:, i, :], xp[r0:r0 + P, :]).then_inc(x_in[i], 16)
            sp.dma_start(x_tok[0:LASTP, 4, :], xp[SEQ - LASTP:SEQ, :]).then_inc(x_in[4], 16)
            sp.dma_start(x_tok[LASTP:R4, 4, :], xs).then_inc(x_in[4], 16)

            def load_block(where, b, src):
                n = where[0]
                hold(sp, lo_done, n + 1)
                sp.dma_start(w_raw[b % 2], src).then_inc(raw_in[b % 2], 16)

            with sp.Fori(0, 4) as t:
                for j in range(2):
                    for n, col in enumerate((COL_SC, COL_SH, COL_SB)):
                        load_block(s_block(t, 3 * j + n), 3 * j + n, w_in_cols(t * (2 * P) + (col + j * P), P))
            with sp.Fori(0, 8) as f:
                load_block(o1_block(f, 0), 0, w_in_cols(f * P + COL_GSC, P))
                load_block(o1_block(f, 1), 1, cols(ins["w_sc_out"][0], f * P, P))
            hsrc = ins["state_ssm"][0].rearrange("b h p n -> b (h p) n")
            hdst = outs[5][0].rearrange("b h p n -> b (h p) n")

            def load_cb(g):
                load_block(g_block(g, 0), 0, w_in_cols(g * P + (COL_X + INNER + GROUPS * NST), P))
                load_block(g_block(g, 1), 1, w_in_cols(g * P + (COL_X + INNER), P))

            def load_gates(t):
                for j in range(2):
                    load_block(o2_block(t, j), j, w_in_cols(t * (2 * P) + (COL_GSSD + j * P), P))

            def load_group(g, last):
                for k in range(GK):
                    load_block(g_block(g, 2 + k), k, w_in_cols(g * GW + (COL_X + k * P), P))
                hold(sp, hs_out, g * 64 + 1)
                for k in range(GK):
                    sp.dma_start(hs[:, k], hsrc[:, bass.ds(g * GW + k * P, P), :].rearrange("b p n -> p b n")
                                 ).then_inc(hs_in, 16)
                for k in range(GK):
                    load_block(g_block(g, 6 + k), k, w_in_cols(g * GW + (COL_Z + k * P), P))
                if last:
                    load_gates(0)
                else:
                    load_cb(g + 1)
                hold(sp, s_hs, g * 4 + 4)
                for k in range(GK):
                    sp.dma_start(hdst[:, bass.ds(g * GW + k * P, P), :].rearrange("b p n -> p b n"), hs[:, k]
                                 ).then_inc(hs_out, 16)

            load_cb(0)
            with sp.Fori(0, GROUPS - 1) as g:
                load_group(g, False)
            load_group(GROUPS - 1, True)
            def load_mixers(t):
                for b in range(2, 6):
                    f, n = b // 2 - 1, b % 2
                    load_block(o2_block(t, b), b, cols(ins["w_ssd_out"][0][n * D:(n + 1) * D, :], t * (2 * P) + f * P, P))

            with sp.Fori(0, 3) as t:
                load_mixers(t)
                load_gates(t + 1)
            load_mixers(3)
            sp.wait_ge(w_done, BLOCKS + 1)
            sp.wait_ge(o_m, 17)
            sp.dma_start(x2[0:N_META, 0, :], meta).then_inc(x_again, 16)
            sp.dma_start(x2[N_META:P, 0, :], xp[0:P - N_META, :]).then_inc(x_again, 16)
            sp.dma_start(x2[:, 1:4, :], xp[P - N_META:4 * P - N_META, :].rearrange("(i p) d -> p i d", p=P)).then_inc(x_again, 16)
            sp.dma_start(x2[0:LASTP, 4, :], xp[SEQ - LASTP:SEQ, :]).then_inc(x_again, 16)
            sp.dma_start(x2[LASTP:R4, 4, :], xs).then_inc(x_again, 16)
            sp.dma_start(wo[1], cols(ins["w_o"][0], 512, 512)).then_inc(wo_in[1], 16)
            sp.dma_start(ln2b, ins["ln2_w"].broadcast_to([P, D])).then_inc(row_in, 16)
            sp.dma_start(fnb, ins["final_norm_w"].unsqueeze(0).broadcast_to([P, D])).then_inc(row_in, 16)
            sp.dma_start(router_w[:, :, 0:NEG], ins["w_rg"][0].rearrange("(k p) f -> p k f", p=P)).then_inc(row_in, 16)
            sp.dma_start(router_w[:, :, NEG:NEG + NE], ins["w_re"][0].rearrange("(k p) f -> p k f", p=P)).then_inc(row_in, 16)
            sp.dma_start(router_b[:, 0:NEG], ins["b_rg"].broadcast_to([P, NEG])).then_inc(row_in, 16)
            sp.dma_start(router_b[:, NEG:NEG + NE], ins["b_re"].broadcast_to([P, NE])).then_inc(row_in, 16)
            sp.wait_ge(r_const, 1)
            sp.dma_start(id_tab.rearrange("(p a) b -> p (a b)", p=P), zero).then_inc(id_zero, 16)

            wg = ins["w_gate"][0].rearrange("a e (p k) f -> (a e) p k f", k=8)
            wu = ins["w_up"][0].rearrange("a e (p k) f -> (a e) p k f", k=8)
            wd = ins["w_down"][0].rearrange("a e (t p) d -> (a e) p t d", p=P)

            def load_expert(e, u, done_sem):
                for part, w in zip(wexp[u], (wg, wu, wd)):
                    src = w[e] if isinstance(e, int) else w[bass.ds(e, 1)].rearrange("o p k f -> (o p) k f")
                    sp.dma_start(part, src).then_inc(done_sem, 16)

            load_expert(0, 0, e_in[0])
            load_expert(3, 3, e_in[3])
            sp.wait_ge(r_mm, TILES)
            load_expert(1, 1, e_in[1])
            load_expert(2, 2, e_in[2])
            with sp.Fori(0, NE // UNROLL - 1) as t:
                for u in range(UNROLL):
                    hold(sp, e_done[u], t + 1)
                    load_expert(t * UNROLL + (UNROLL + u), u, e_in[u])
            sp.wait_ge(r_ids, 1)
            sp.wait_ge(m_dn, NE)
            n_most = sp.value_load(most[0:1, 0:1], min_val=0, max_val=T)
            with sp.If(n_most > CAP):
                sp.wait_ge(r_tab, 16 * 2 * TILES)
                with sp.Fori(0, NE) as e:
                    with sp.Fori(0, ROUNDS) as r:
                        n = e * ROUNDS + r
                        hold(sp, f_out, n * 16 + 1)
                        load_expert(e, 0, f_w)
                        sp.dma_start(idf[:, :], id_tab[bass.ds(e * SLOTS + r * CAP + CAP, CAP), :]).then_inc(f_id, 16)
            yp, ys = outs[0][0], outs[1].rearrange("b s d -> (b s) d")
            for i in range(TILES):
                sp.wait_ge(z_y, i + 1)
                if i == 0:
                    sp.dma_start(yp[0:P - N_META, :], x2[N_META:P, 0, :]).then_inc(y_out, 16)
                elif i < 4:
                    sp.dma_start(yp[i * P - N_META:(i + 1) * P - N_META, :], x2[:, i, :]).then_inc(y_out, 16)
                else:
                    sp.dma_start(yp[SEQ - LASTP:SEQ, :], x2[0:LASTP, 4, :]).then_inc(y_out, 16)
                    sp.dma_start(ys, x2[LASTP:R4, 4, :]).then_inc(y_out, 16)
            sp.wait_ge(y_out, 16 * 6)
            sp.wait_ge(tails_out, 16 * 4)


        def pe_block(pe, where, b, hi, lo, first=True, last=True, part=None):
            n_, _, a, ause = where
            s = b % 2
            if part in (None, 0):
                pe.wait_ge(lo_done, n_ + 3)
                if first:
                    pe.wait_ge(acc_free[a], ause + 1)
            m = None
            for k in range(8):
                for w, x in ((w_hi, hi), (w_hi, lo), (w_lo, hi)):
                    for h in (range(2) if part is None else (part,)):
                        n = HALF if h == 0 else T - HALF
                        m = nc.tensor.matmul(acc[a][:, h, 0:n], w[s][:, k, :], x[:, k, h * HALF:h * HALF + n],
                                             start=first and k == 0 and w is w_hi and x is hi,
                                             stop=last and k == 7 and w is w_lo)
            if part in (None, 1):
                m.then_inc(w_done, 1)

        @block.tensor
        def _(pe):
            pe.wait_ge(consts, 1)
            pe.sem_inc(p_seg, 2)
            pe.sem_inc(p_y, 1)
            pe.sem_inc(p_yb, 2)
            pe.sem_inc(w_done, 1)
            pe.wait_ge(v1_in, 16 * 3)
            for k in range(8):
                m = nc.tensor.transpose(pT[:, 20 * k:20 * k + 20], v1[0:20, k * P:(k + 1) * P], ident[0:20, 0:20])
            m.then_inc(s_vtr, 1)
            for i in range(TILES):
                pe.wait_ge(s_htok, i + 1)
                if i >= 2:
                    pe.wait_ge(s_hT, i - 1)
                a = acc[i % 2].rearrange("p a b -> p (a b)")
                for k in range(8):
                    m = nc.tensor.transpose(a[:, k * P:k * P + ROWS[i]], h_tok[0:ROWS[i], i % 2, k * P:(k + 1) * P],
                                            ident[0:ROWS[i], 0:ROWS[i]])
                m.then_inc(s_htr, 1)
            pe.wait_ge(s_hT, TILES)
            pe.wait_ge(vec_in, 16 * 8)
            for i in range(TILES):
                for k in range(8):
                    m = nc.tensor.matmul(pO[0:ROWS[i], i * HEADS:(i + 1) * HEADS], hT[:, k, tok(i)], wdt[:, k, :],
                                         start=k == 0, stop=k == 7)
            m.then_inc(s_dtmm, 1)
            pe.wait_ge(vec_in, 16 * 8)
            pe.wait_ge(s_dexp, 1)
            for k in range(16):
                m = nc.tensor.transpose(pT[:, 160 + 2 * k:162 + 2 * k], v2[0:2, k * P:(k + 1) * P], ident[0:2, 0:2])
            pe.wait_ge(s_vcp, 1)
            for k in range(XT_TILES):
                bank_ = pY if k < 12 else pS
                m = nc.tensor.transpose(bank_[:, 29 * (k % 12):29 * (k % 12) + 29], v3[0:29, k * P:(k + 1) * P], ident[0:29, 0:29])
            m.then_inc(s_vtr, 1)
            pe.wait_ge(h_lo, TILES)
            with pe.Fori(0, 4) as t:
                for b in range(6):
                    pe_block(pe, s_block(t, b), b, hT_hi, hT_lo)
            pe.wait_ge(s_dtv, 3)
            pe.wait_ge(s_vcp, 4)
            for i in range(TILES):
                r = ROWS[i]
                le, gt = (m_le, m_gt) if i < 4 else (m_le4, m_gt4)
                last_prompt = P if i < 4 else LASTP
                d_i = da[0:r, i, :]
                nc.tensor.matmul(pY[0:r, i * 32:i * 32 + 32], le[0:r, 0:r], d_i, start=True, stop=True)
                nc.tensor.matmul(pY[0:r, 160 + i * 32:192 + i * 32], gt[0:r, 0:r], d_i, start=True, stop=True)
                nc.tensor.matmul(pY[:, 320 + i * 32:352 + i * 32], ones[0:last_prompt, :], da[0:last_prompt, i, :],
                                 start=True, stop=True)
            nc.tensor.matmul(pS[0:R4, 0:HEADS], m_blk4[:, :], da[0:R4, 4, :], start=True, stop=True).then_inc(s_cum, 1)
            with pe.Fori(0, 8) as f:
                pe_block(pe, o1_block(f, 0), 0, hT_hi, hT_lo)
                pe.wait_ge(s_sco, 8)
                pe_block(pe, o1_block(f, 1), 1, sco_hi, sco_lo)
            pe.wait_ge(s_dta, 7)
            pe_block(pe, g_block(0, 0), 0, hT_hi, hT_lo)
            with pe.Fori(0, GROUPS) as g:
                for b in range(1, 7):
                    pe_block(pe, g_block(g, b), b, hT_hi, hT_lo)
                pe.wait_ge(s_silu, g * 6 + 8)
                pe.wait_ge(s_rm, g + 1)
                for i in range(TILES):
                    r = ROWS[i]
                    le, gt = (m_le, m_gt) if i < 4 else (m_le4, m_gt4)
                    for k in range(GK):
                        m = nc.tensor.transpose(pT[0:r, k * P:(k + 1) * P], xT[:, k, tok(i)], ident[:, :])
                    m.then_inc(p_xt, 1)
                    pe.wait_ge(s_y1, g * 5 + (i + 1))
                    nc.tensor.matmul(pO[0:r, 0:r], bT[:, tok(i)], cT[:, tok(i)], start=True, stop=True)
                    nc.tensor.transpose(pO[0:r, P:2 * P], bT[:, tok(i)], ident[:, :]).then_inc(p_cb, 1)
                    for q in range(2):
                        if q == 1 and i < 3:
                            pe_block(pe, g_block(g, 7 + i), 7 + i, hT_hi, hT_lo, part=0)
                        pe.wait_ge(s_r, g * 10 + (2 * i + q + 1))
                        pe.wait_ge(s_exp, g * 10 + (2 * i + q + 1))
                        if q == 0:
                            pe.wait_ge(s_st, g * 6 + (i + 1))
                        nc.tensor.matmul(pS[0:r, 0:4 * r], gt[0:r, 0:r], rbuf[0:r, q, 0:4 * r],
                                         start=True, stop=True).then_inc(p_seg, 1)
                    pe.wait_ge(s_cb, g * 5 + (i + 1))
                    pe.wait_ge(s_bt, g * 5 + (i + 1))
                    if i < 4:
                        nc.tensor.matmul(pO[0:r, :], cT[:, tok(i)], st, start=True, stop=True).then_inc(p_yo, 1)
                    else:
                        pe.wait_ge(s_xd, g * 5 + 5)
                        pe.wait_ge(s_dx, g + 1)
                        for k in range(GK):
                            m = nc.tensor.matmul(pT[:, k * 8:k * 8 + 8], dx[0:R4, k * P:(k + 1) * P],
                                                 ident[0:R4, LASTP:R4:SLEN], start=True, stop=True)
                        m.then_inc(p_df, 1)
                        pe.wait_ge(hs_in, g * 64 + 64)
                        pe.wait_ge(acc_free[0], g * 5 + 26)
                        pe.wait_ge(acc_free[1], g * 5 + 26)

                        def h0_transpose(b):
                            if b >= 4:
                                pe.wait_ge(s_h0, g * 8 + (b - 3))
                            for k in range(GK):
                                m = nc.tensor.transpose(acc[b % 4 // 2][:, b % 2, k * P:(k + 1) * P], hs[:, k, b, :],
                                                        ident[:, :])
                            m.then_inc(p_h0, 1)

                        h0_transpose(0)
                        h0_transpose(1)
                        pe.wait_ge(s_cm, g + 1)
                        nc.tensor.matmul(pO[0:r, :], cmask[:, 0:R4], st, start=True, stop=False)
                        for b in range(NSEQ):
                            pe.wait_ge(s_h0, g * 8 + (b + 1))
                            nc.tensor.matmul(pO[0:r, :], cmask[:, (b + 1) * R4:(b + 2) * R4], h0T[:, b % 2, :],
                                             start=False, stop=b == NSEQ - 1).then_inc(p_yb, 1)
                            if b + 2 < NSEQ:
                                h0_transpose(b + 2)
                    if i < 3:
                        pe_block(pe, g_block(g, 7 + i), 7 + i, hT_hi, hT_lo, part=1)
                    pe.wait_ge(s_xd, g * 5 + (i + 1))
                    pe.wait_ge(s_w, g * 10 + (2 * i + 2))
                    pe.wait_ge(s_u, g * 5 + (i + 1))
                    for h in range(HPG):
                        m = nc.tensor.matmul(pY[0:r, h * HD:(h + 1) * HD], wts[0:r, h // 4, (h % 4) * r:(h % 4 + 1) * r],
                                             xdt[0:r, i % 2, h * HD:(h + 1) * HD], start=True, stop=True)
                    m.then_inc(p_y, 1)
                    kk = r if i < 4 else LASTP
                    pe.wait_ge(s_exp, g * 10 + (2 * i + 3))
                    nc.tensor.matmul(pS[:, :], btok[0:kk, i % 2, :], xte[0:kk, i % 2, :], start=True, stop=True
                                     ).then_inc(p_sn, 1)
                    if i == 4:
                        pe.wait_ge(s_bm, g + 1)
                        for k in range(GK):
                            if k >= 2:
                                pe.wait_ge(s_hs, g * 4 + (k - 1))
                            for h in range(2):
                                m = nc.tensor.matmul(acc[k % 2][:, h, :], xte[0:R4, 0, k * P:(k + 1) * P],
                                                     bmask[0:R4, 4 * h:4 * h + 4, :], start=True, stop=True)
                            m.then_inc(p_hs, 1)
                    pe.wait_ge(s_y2, g * 5 + (i + 2))
                    if i == 4:
                        pe.wait_ge(s_df, g + 1)
                    for k in range(GK):
                        m = nc.tensor.transpose(pY[:, k * P:k * P + r], ytok[0:r, k * P:(k + 1) * P], ident[0:r, 0:r])
                    m.then_inc(p_yt, 1)
                pe.wait_ge(s_st, g * 6 + 6)
                for k in range(GK):
                    m = nc.tensor.transpose(pT[:, k * P:(k + 1) * P], st[:, k * P:(k + 1) * P], ident[:, :])
                m.then_inc(p_so, 1)
                pe.wait_ge(s_hs, g * 4 + 4)
                pe_block(pe, g_block(g, 10), 10, hT_hi, hT_lo)
                pe.wait_ge(s_so, g + 1)
                pe.wait_ge(s_sq, g + 1)
                for h, pb in ((0, pT), (1, pS)):
                    n = HALF if h == 0 else T - HALF
                    for k in range(GK):
                        m = nc.tensor.matmul(pb[:, 0:n], ones[:, :], sq[:, k, h * HALF:h * HALF + n],
                                             start=k == 0, stop=k == GK - 1)
                m.then_inc(p_gn, 1)
            def mixer_turn(t, last):
                pe_block(pe, o2_block(t, 1), 1, hT_hi, hT_lo)
                for b in range(2, 6):
                    n = b % 2
                    pe.wait_ge(h_lo, TILES + 1)
                    pe.wait_ge(u_lo, 1 + 2 * n)
                    pe_block(pe, o2_block(t, b), b, uT_hi[:, 8 * n:8 * n + 8, :], uT_lo[:, 8 * n:8 * n + 8, :],
                             first=n == 0, last=n == 1)
                if not last:
                    pe_block(pe, o2_block(t, 6), 6, hT_hi, hT_lo)

            with pe.Fori(0, 3) as t:
                mixer_turn(t, False)
            mixer_turn(3, True)
            pe.wait_ge(o_m, 16)
            for h in range(2):
                pe.wait_ge(wo_in[h], 16)
                for i in range(TILES):
                    n = h * TILES + i
                    if n >= 4:
                        pe.wait_ge(r_x2, n - 3)
                    for k in range(8):
                        if n == 0 and k == 7:
                            pe.wait_ge(o_m, 17)
                        m = nc.tensor.matmul(acc[n % 4 // 2][0:ROWS[i], n % 2, :], mT[:, k, tok(i)], wo[h][:, k, :],
                                             start=k == 0, stop=k == 7)
                    m.then_inc(r_mm, 1)
            pe.wait_ge(row_in, 16 * 6)
            pe.wait_ge(r_x2, 2 * TILES)

            def logits(i):
                r = ROWS[i]
                pe.wait_ge(r_h2T, i + 1)
                for k in range(8):
                    m = nc.tensor.matmul(pY[0:r, i * 36:i * 36 + 36], h2T[:, i % 2, k, 0:r], router_w[:, k, :],
                                         start=k == 0, stop=k == 7)
                m.then_inc(r_lg, 1)

            for i in range(TILES):
                r = ROWS[i]
                pe.wait_ge(r_h2, i + 1)
                if i >= 2:
                    pe.wait_ge(r_h2T, i - 1)
                a = acc[i % 2].rearrange("p a b -> p (a b)")
                for k in range(8):
                    m = nc.tensor.transpose(a[:, k * P:k * P + r], h2[0:r, i % 2, k * P:(k + 1) * P], ident[0:r, 0:r])
                m.then_inc(r_tr, 1)
                if i >= 1:
                    logits(i - 1)
            logits(TILES - 1)
            banks = [acc[0][:, 0, :], acc[0][:, 1, :], acc[1][:, 0, :], acc[1][:, 1, :]]
            for n in range(8):
                if n >= 4:
                    pe.wait_ge(s_tl, n - 3)
                for k in range(4):
                    if n < 6:
                        c = n * 4 + k
                        m = nc.tensor.transpose(banks[n % 4][0:TAIL, k * P:(k + 1) * P], xtail[:, c, :], ident[:, :])
                    else:
                        m = nc.tensor.transpose(banks[n % 4][0:STAIL, k * P:(k + 1) * P], stail[:, (n - 6) * 4 + k, :],
                                                ident[:, :])
                m.then_inc(p_tl, 1)
            pe.wait_ge(r_hot, 1)
            for i in range(TILES):
                r = ROWS[i]
                if i >= 1:
                    nc.tensor.matmul(pO[0:r, i * NE:(i + 1) * NE], ones[:, 0:r], before[:, i - 1, :], start=True, stop=False)
                m = nc.tensor.matmul(pO[0:r, i * NE:(i + 1) * NE], m_lt[0:r, 0:r], mm[0:r, i, :], start=i == 0, stop=True)
            m.then_inc(r_pos, 1)
            pe.wait_ge(r_sel, 1)
            for i in range(TILES):
                for n in range(2):
                    m = nc.tensor.matmul(pS[0:CAP, 0:NE], at_slot[0:ROWS[i], n * TILES + i, :], tok_of[0:ROWS[i], n * TILES + i, :],
                                         start=i + n == 0, stop=i == TILES - 1 and n == 1)
            m.then_inc(r_idtr, 1)
            nc.tensor.matmul(pY[:, 192:192 + NE], ones[:, :], before[:, TILES - 2, :], start=True, stop=False)
            nc.tensor.matmul(pY[:, 192:192 + NE], ones[0:R4, :], mm[0:R4, TILES - 1, :], start=False, stop=True).then_inc(r_pos, 1)

            def to_rows(u, s):
                for k in range(8):
                    m = nc.tensor.transpose(acc[0][:, k // 4, (k % 4) * CAP:(k % 4 + 1) * CAP],
                                            xe[u][0:CAP, k:D:8], ident[0:CAP, 0:CAP])
                m.then_inc(s, 1)

            def gate_up(u, uu, bank_, s):
                for n, w in ((0, wexp[u][0]), (1, wexp[u][1])):
                    for ft in range(FK):
                        for k in range(8):
                            m = nc.tensor.matmul(bank_[:, (n * FK + ft) * CAP:(n * FK + ft + 1) * CAP],
                                                 w[:, k, ft * P:(ft + 1) * P], xeT[uu][:, k, :], start=k == 0, stop=k == 7)
                m.then_inc(s, 1)

            def down(u, uu, banks_, s):
                for h in range(2):
                    for ft in range(FK):
                        m = nc.tensor.matmul(banks_[h], gs[uu][:, ft, :], wexp[u][2][:, ft, h * 512:(h + 1) * 512],
                                             start=ft == 0, stop=ft == FK - 1)
                m.then_inc(s, 1)

            down_banks = [(acc[1][0:CAP, 0, :], acc[1][0:CAP, 1, :]), (pY[0:CAP, :], pO[0:CAP, :])]
            pe.wait_ge(r_ids, 1)
            pe.wait_ge(xe_in[0], 16)
            pe.wait_ge(s_tl, 8)
            to_rows(0, m_tr)
            with pe.Fori(0, NE // UNROLL) as t:
                for u in range(UNROLL):
                    e = t * UNROLL + u
                    pe.wait_ge(e_in[u], t * 48 + 48)
                    pe.wait_ge(m_xe, e + 1)
                    gate_up(u, u % 2, pS if u % 2 else pT, m_gu)
                    un = (u + 1) % UNROLL
                    pe.wait_ge(xe_in[un], t * 16 + (32 if un == 0 else 16))
                    to_rows(un, m_tr)
                    pe.wait_ge(m_act, e + 1)
                    pe.wait_ge(m_ye, e + 1)
                    down(u, u % 2, down_banks[u % 2], e_done[u])
            pe.wait_ge(m_xe, NE + 1)
            pe.wait_ge(m_ye, NE + 1)
            pe.wait_ge(r_slot, 1)
            pe.sem_inc(m_dn, NE)
            n_most = pe.value_load(most[0:1, 0:1], min_val=0, max_val=T)
            with pe.If(n_most > CAP):
                with pe.Fori(0, NE) as e:
                    with pe.Fori(0, ROUNDS) as r:
                        n = e * ROUNDS + r
                        pe.wait_ge(f_x, n * 16 + 16)
                        to_rows(0, f_tr)
                        pe.wait_ge(f_w, n * 48 + 48)
                        pe.wait_ge(f_xe, n + 1)
                        gate_up(0, 0, pT, f_gu)
                        pe.wait_ge(f_act, n + 1)
                        down(0, 0, down_banks[0], f_dn)

        @block.vector
        def _(dve):
            v = nc.vector
            link = chain(dve, dve_chain, 0)
            dve.sem_inc(s_u, 1)
            dve.sem_inc(s_y1, 1)
            dve.sem_inc(s_y2, 1)
            dve.sem_inc(s_cvd, 2)
            dve.sem_inc(c_conv, 2)
            dve.sem_inc(o_m, 1)
            dve.sem_inc(m_ye, 1)
            link(v.memset(pO[:, 0:160], 0.0))
            link(v.memset(pY[:, 0:480], 0.0))
            def to_features(i):
                dve.wait_ge(s_htr, i + 1)
                a = acc[i % 2].rearrange("p a (c b) -> p (a c) b", b=P)
                v.tensor_tensor(hT[:, :, tok(i)], a[:, :, 0:ROWS[i]],
                                svec[:, :, 19:20].broadcast_to([P, 8, ROWS[i]]), ALU.mult).then_inc(s_hT, 1)

            for i in range(TILES):
                r = ROWS[i]
                dve.wait_ge(s_sd, i + 1)
                link(v.reciprocal(stat[0:r, 2, i:i + 1], stat[0:r, 1, i:i + 1]))
                if i >= 2:
                    dve.wait_ge(s_htr, i - 1)
                v.tensor_scalar(h_tok[0:r, i % 2, :], x_tok[0:r, i, :], stat[0:r, 2, i:i + 1], None, ALU.mult
                                ).then_inc(s_htok, 1)
                if i == 0:
                    dve.wait_ge(s_vtr, 1)
                    v.tensor_copy(svec.rearrange("p a b -> p (a b)"), pT[:, 0:160]).then_inc(s_vcp, 1)
                    dve.wait_ge(s_vcp, 1)
                else:
                    to_features(i - 1)
            to_features(TILES - 1)
            dve.wait_ge(vec_in, 16 * 8)
            v.tensor_copy(v2[0:1, :].rearrange("p (h c) -> p h c", c=HD),
                          drow[0:1, :].unsqueeze(2).broadcast_to([1, HEADS, HD])).then_inc(s_dexp, 1)
            x_, ab, e_, u_, l_, z_ = (dtw[:, n, :] for n in range(6))
            dve.wait_ge(s_dtmm, 1)
            link(v.tensor_tensor(x_.rearrange("p (i h) -> p i h", h=HEADS), pO[:, 0:160].rearrange("p (i h) -> p i h", h=HEADS),
                                 dtb.unsqueeze(1).broadcast_to([P, TILES, HEADS]), ALU.add))
            v.scalar_tensor_tensor(ab, x_, -1.0, x_, ALU.mult, ALU.max).then_inc(s_dtv, 1)
            dve.wait_ge(s_dta, 1)
            v.tensor_scalar(u_, e_, 1.0, None, ALU.add).then_inc(s_dtv, 1)
            dve.wait_ge(s_dtv, 2)
            link(v.tensor_scalar(ab, u_, -1.0, None, ALU.add))
            link(v.tensor_scalar(z_, ab, 0.0, None, ALU.is_equal))
            link(v.tensor_tensor(ab, ab, z_, ALU.add))
            link(v.reciprocal(ab, ab))
            dve.wait_ge(s_dta, 2)
            link(v.tensor_tensor(l_, l_, ab, ALU.mult))
            link(v.tensor_tensor(l_, l_, z_, ALU.add))
            link(v.tensor_tensor(l_, l_, e_, ALU.mult))
            flat = dt_.rearrange("p i h -> p (i h)")
            link(v.scalar_tensor_tensor(flat, x_, 0.0, l_, ALU.max, ALU.add))
            dve.wait_ge(s_dta, 3)
            v.scalar_tensor_tensor(da[:, :, :], dt_[:, :, :], -1.0, ea.unsqueeze(1).broadcast_to([P, TILES, HEADS]),
                                   ALU.mult, ALU.mult).then_inc(s_dtv, 1)
            start = link.count[0]
            dve.wait_ge(s_vtr, 2)
            v.tensor_copy(dnv.rearrange("p a b -> p (a b)"), pT[:, 160:192]).then_inc(s_vcp, 1)
            for h, bank_ in ((0, pY), (1, pS)):
                v.tensor_copy(xvec[:, 12 * h:12 * h + 12, :].rearrange("p a b -> p (a b)"), bank_[:, 0:348]).then_inc(s_vcp, 1)
            with dve.Fori(0, 4) as t:
                link2 = chain(dve, dve_chain, start, t, 10)
                for j in range(2):
                    dve.wait_ge(c_tail, t * 2 + (j + 1))
                    puse, _, pa, pause = s_block(t, 3 * j + 1)
                    dve.wait_ge(w_done, puse + 2)
                    _, _, sa, sause = s_block(t, 3 * j)
                    dve.wait_ge(acc_free[sa], sause + 2)
                    a0, a1 = acc_parts(acc[pa])
                    c0, c1 = halves(s_c[:, j, :])
                    d0, d1 = pad_parts(s_pad[:, j, :], SH, SROW)
                    link2(v.tensor_tensor(d0, a0, c0, ALU.mult))
                    v.tensor_tensor(d1, a1.rearrange(seqs, c=SLEN), c1.rearrange(seqs, c=SLEN), ALU.mult
                                    ).then_inc(acc_free[pa], 1)
                    dve.wait_ge(acc_free[pa], pause + 2)
                    dve.wait_ge(c_hist, t * 2 + (j + 1))
                    wv = svec[:, bass.ds(t * 2 + j, 1), 0:3]
                    link2(v.tensor_scalar(s_cv[:, j, 0:SCONV], s_pad[:, j, 0:SCONV], wv[:, 0, 0:1], None, ALU.mult))
                    link2(v.scalar_tensor_tensor(s_cv[:, j, 0:SCONV], s_pad[:, j, 1:1 + SCONV], wv[:, 0, 1:2], s_cv[:, j, 0:SCONV],
                                                 ALU.mult, ALU.add))
                    v.scalar_tensor_tensor(s_cv[:, j, 0:SCONV], s_pad[:, j, 2:2 + SCONV], wv[:, 0, 2:3], s_cv[:, j, 0:SCONV],
                                           ALU.mult, ALU.add).then_inc(c_conv, 1)
                    dve.wait_ge(c_conv, t * 2 + (j + 3))
                    buse, _, ba, bause = s_block(t, 3 * j + 2)
                    dve.wait_ge(w_done, buse + 2)
                    a0, a1 = acc_parts(acc[ba])
                    g0, g1 = halves(s_o[:, j, :])
                    v0, v1_ = conv_parts(s_cv[:, j, :], SH, SROW)
                    link2(v.tensor_tensor(g0, a0, v0, ALU.mult))
                    v.tensor_tensor(g1.rearrange(seqs, c=SLEN), a1.rearrange(seqs, c=SLEN), v1_, ALU.mult
                                    ).then_inc(acc_free[ba], 1)
                    dve.wait_ge(acc_free[ba], bause + 2)
                    of = lambda x: x[:, bass.ds(t * 2 + j, 1), :].rearrange("p a b -> p (a b)")
                    link2(v.tensor_copy(of(sco_hi), s_o[:, j, :]))
                    v.tensor_tensor(of(sco_lo), s_o[:, j, :], of(sco_hi).bitcast(F32), ALU.subtract).then_inc(s_sco, 1)
                assert link2.count[0] == 10, link2.count
            start += 4 * 10
            dve.wait_ge(s_dta, 5)
            link = chain(dve, dve_chain, start)
            link(v.tensor_tensor(dte[:, :, :], dte[:, :, :], dt_[:, :, :], ALU.mult))
            start += 1
            with dve.Fori(0, 8) as f:
                use, _, a, ause = o1_block(f, 1)
                dve.wait_ge(o_sg, f + 1)
                dve.wait_ge(w_done, use + 2)
                a0, a1 = acc_parts(acc[a])
                g0, g1 = halves(sg[:, 0, :])
                m0, m1_ = halves(mT[:, bass.ds(f, 1), :].rearrange("p a b -> p (a b)"))
                v.tensor_tensor(m0, a0, g0, ALU.mult)
                v.tensor_tensor(m1_, a1, g1, ALU.mult).then_inc(acc_free[a], 1)
                dve.wait_ge(acc_free[a], ause + 2)
                dve.sem_inc(o_m, 1)
            with dve.Fori(0, GROUPS) as g:
                link = chain(dve, dve_chain, start, g, 25)
                link(v.tensor_copy(dg[:, :, :], dnv[:, bass.ds(g * GK, GK), :]))
                v.memset(st, 0.0).then_inc(s_st, 1)
                for c in range(6):
                    _, _, a, ause = g_block(g, c)
                    dve.wait_ge(acc_free[a], ause + 2)
                    dve.wait_ge(s_hist, g * 6 + (c + 1))
                    dve.wait_ge(s_silu, g * 6 + (c + 1))
                    w = xvec[:, bass.ds(conv_tile(g, c), 1), 0:4]
                    o_ = cv[:, c % 2, 0:XCONV]
                    link(v.tensor_scalar(o_, raw[:, c % 2, 0:XCONV], w[:, 0, 0:1], None, ALU.mult))
                    for n in range(1, 4):
                        x = v.scalar_tensor_tensor(o_, raw[:, c % 2, n:n + XCONV], w[:, 0, n:n + 1], o_, ALU.mult, ALU.add)
                        if n < 3:
                            link(x)
                    x.then_inc(s_cvd, 1)
                for i in range(TILES):
                    r = ROWS[i]
                    heads = bass.ds(g * HPG, HPG)

                    def per_head(src, n=HD):
                        return src[0:r, i, heads].unsqueeze(2).broadcast_to([r, HPG, n])

                    byhead = "p (h c) -> p h c"
                    dve.wait_ge(p_xt, g * 5 + (i + 1))
                    x_i = pT[0:r, :].rearrange(byhead, c=HD)
                    v.tensor_tensor(xdt[0:r, i % 2, :].rearrange(byhead, c=HD), x_i, per_head(dt_), ALU.mult)
                    v.tensor_tensor(xte[0:r, i % 2, :].rearrange(byhead, c=HD), x_i, per_head(dte), ALU.mult
                                    ).then_inc(s_xd, 1)
                    if i == 4:
                        v.tensor_copy(dx[0:R4, :].rearrange(byhead, c=HD),
                                      sdec[:, heads].unsqueeze(2).broadcast_to([R4, HPG, HD])).then_inc(s_dx, 1)
                    dve.wait_ge(s_bt, g * 5 + (i + 1))
                    le = m_le if i < 4 else m_le4
                    v.tensor_tensor(cbm[0:r, 0:r], pO[0:r, 0:r], le[0:r, 0:r], ALU.mult).then_inc(s_cb, 1)
                    dve.wait_ge(s_cb, g * 5 + (i + 1))
                    if i == 4:
                        dve.wait_ge(p_df, g + 1)
                        v.tensor_copy(df[:, :, :].rearrange("p k s -> p (k s)"), pT[:, 0:32]).then_inc(s_df, 1)
                    for q in range(2):
                        dve.wait_ge(s_exp, g * 10 + (2 * i + q + 2))
                        w = wts[0:r, q, 0:4 * r].rearrange("p (h c) -> p h c", h=4)
                        v.tensor_tensor(w, w, cbm[0:r, 0:r].unsqueeze(1).broadcast_to([r, 4, r]), ALU.mult
                                        ).then_inc(s_w, 1)
                    if i < 4:
                        dve.wait_ge(p_yo, g * 4 + (i + 1))
                    else:
                        dve.wait_ge(p_yb, g * 8 + 10)
                    y_i = ytok[0:r, :].rearrange(byhead, c=HD)
                    v.tensor_tensor(y_i, pO[0:r, :].rearrange(byhead, c=HD), per_head(e_acum), ALU.mult).then_inc(s_y1, 1)
                    st_v = st.rearrange(byhead, c=HD)
                    link(v.tensor_tensor(st_v, st_v, dec[:, i, heads].unsqueeze(2).broadcast_to([P, HPG, HD]), ALU.mult))
                    dve.wait_ge(s_y1, g * 5 + (i + 2))
                    dve.wait_ge(p_y, g * 5 + (i + 2))
                    v.tensor_tensor(ytok[0:r, :], ytok[0:r, :], pY[0:r, :], ALU.add).then_inc(s_y2, 1)
                    dve.wait_ge(p_sn, g * 5 + (i + 1))
                    v.tensor_tensor(st, st, pS[:, :], ALU.add).then_inc(s_st, 1)
                    if i == 4:
                        for k in range(GK):
                            dve.wait_ge(p_hs, g * 4 + (k + 1))
                            dve.wait_ge(s_hd, g * 4 + (k + 1))
                            h_k = hs[:, k, :, :].rearrange("p s n -> p (s n)")
                            v.tensor_tensor(h_k, h_k, acc[k % 2].rearrange("p a b -> p (a b)"), ALU.add).then_inc(s_hs, 1)
                    dve.wait_ge(p_yt, g * 5 + (i + 1))
                    for k in range(GK):
                        u_k = uT[:, bass.ds(g * GK + k, 1), tok(i)].rearrange("p a b -> p (a b)")
                        x = v.scalar_tensor_tensor(u_k, xT[:, k, tok(i)], dg[:, k, 0:1], pY[:, k * P:k * P + r],
                                                   ALU.mult, ALU.add)
                    x.then_inc(s_u, 1)
                dve.wait_ge(s_sz, g + 1)
                dve.wait_ge(s_u, g * 5 + 6)
                u_g = uT[:, bass.ds(g * GK, GK), :]
                v.tensor_tensor(u_g, u_g, sz, ALU.mult).then_inc(s_uz, 1)
                dve.wait_ge(s_rm, g + 2)
                link(v.reciprocal(rms, rms))
                for k in range(GK):
                    u_k = uT[:, bass.ds(g * GK + k, 1), :].rearrange("p a b -> p (a b)")
                    x = v.scalar_tensor_tensor(u_k, u_k, dg[:, k, 1:2], rms, ALU.mult, ALU.mult)
                x.then_inc(s_un, 1)
                dve.wait_ge(s_un, g + 1)
                assert link.count[0] == 25, link.count
            start += GROUPS * 25
            for c in range(1, 4):
                u_c = uT[:, 4 * c:4 * c + 4, :]
                dve.wait_ge(u_hi, c + 1)
                v.tensor_tensor(uT_lo[:, 4 * c:4 * c + 4, :], u_c, uT_hi[:, 4 * c:4 * c + 4, :].bitcast(F32), ALU.subtract
                                ).then_inc(u_lo, 1)
            with dve.Fori(0, 4) as t:
                link = chain(dve, dve_chain, start, t, 4)
                for j in range(2):
                    m_f = mT[:, bass.ds(t * 2 + j, 1), :].rearrange("p a b -> p (a b)")
                    use, _, a, ause = o2_block(t, 3 + 2 * j)
                    dve.wait_ge(o_sg, t * 2 + (9 + j))
                    dve.wait_ge(w_done, use + 2)
                    a0, a1 = acc_parts(acc[a])
                    g0, g1 = halves(sg[:, j, :])
                    p0, p1 = halves(sg[:, 2, :])
                    link(v.tensor_tensor(p0, a0, g0, ALU.mult))
                    v.tensor_tensor(p1, a1, g1, ALU.mult).then_inc(acc_free[a], 1)
                    dve.wait_ge(acc_free[a], ause + 2)
                    link(v.tensor_tensor(m_f, m_f, sg[:, 2, :], ALU.add))
                    dve.sem_inc(o_m, 1)
                assert link.count[0] == 4, link.count
            start += 4 * 4
            link = chain(dve, dve_chain, start)

            def normed_row(i):
                r = ROWS[i]
                dve.wait_ge(r_sd, i + 1)
                link(v.reciprocal(stat[0:r, 2, i:i + 1], stat[0:r, 1, i:i + 1]))
                if i >= 2:
                    dve.wait_ge(r_tr, i - 1)
                    dve.wait_ge(h2_out[i % 2], 16 * (i // 2))
                v.scalar_tensor_tensor(h2[0:r, i % 2, :], x2[0:r, i, :], stat[0:r, 2, i:i + 1], ln2b[0:r, :],
                                       ALU.mult, ALU.mult).then_inc(r_h2, 1)

            link(v.memset(pY[:, 0:TILES * 36], 0.0))
            link(v.memset(pO[:, 0:160], 0.0))
            dve.wait_ge(x_again, 16 * 5)
            dve.wait_ge(row_in, 16 * 6)
            for h in range(2):
                for i in range(TILES):
                    n = h * TILES + i
                    r = ROWS[i]
                    dve.wait_ge(r_mm, n + 1)
                    row = x2[0:r, i, h * 512:(h + 1) * 512]
                    v.tensor_tensor(row, row, acc[n % 4 // 2][0:r, n % 2, :], ALU.add).then_inc(r_x2, 1)
                    if h == 1 and i in (2, 3):
                        normed_row(i - 2)
            for i in range(TILES):
                r = ROWS[i]
                if i >= 2:
                    normed_row(i)
                dve.wait_ge(r_tr, i + 1)
                if i >= 2:
                    dve.wait_ge(r_lg, i - 1)
                a = acc[i % 2].rearrange("p a (c b) -> p (a c) b", b=P)
                v.tensor_copy(h2T[:, i % 2, :, 0:r], a[:, :, 0:r]).then_inc(r_h2T, 1)
            dve.wait_ge(r_lg, TILES)
            dve.wait_ge(r_const, 1)
            gm, gsum, gprob, top1, top2, ev, v1s, cmax = (sc[:, n, :] for n in range(8))
            by36 = "p (i c) -> p i c"
            link(v.tensor_tensor(lg, pY[:, 0:TILES * 36].rearrange(by36, c=36), router_b.unsqueeze(1).broadcast_to([P, TILES, 36]),
                                 ALU.add))
            lg_g, lg_e = lg[:, :, 0:NEG], lg[:, :, NEG:NEG + NE]

            def wide(x, n):
                return x.unsqueeze(2).broadcast_to([P, TILES, n])

            def first_of(out, values, best, n, ramp_, tmp, tmpmax):
                link(v.tensor_tensor(out, values, wide(best, n), ALU.is_equal))
                link(v.tensor_tensor(tmp, out, ramp_.unsqueeze(1).broadcast_to([P, TILES, n]), ALU.mult))
                link(v.tensor_reduce(tmpmax, tmp, AX.X, ALU.max))
                link(v.tensor_tensor(out, tmp, wide(tmpmax, n), ALU.is_equal))

            link(v.tensor_reduce(gm, lg_g, AX.X, ALU.max))
            first_of(ohg, lg_g, gm, NEG, ramp[:, 0:NEG], t4, cmax)
            v.tensor_tensor(t4, lg_g, wide(gm, NEG), ALU.subtract).then_inc(r_dve, 1)
            pr_, m1_, m2_ = pr, m1, m2
            link(v.tensor_tensor(pr_, lg_e.rearrange("p i (a b) -> p i a b", a=NEG), ohg.unsqueeze(3).broadcast_to([P, TILES, NEG, EPG]),
                                 ALU.mult))
            link(v.tensor_reduce(le_, pr_.rearrange("p i a b -> p i b a"), AX.X, ALU.add))
            link(v.tensor_reduce(top1, le_, AX.X, ALU.max))
            first_of(oh1, le_, top1, EPG, ramp[:, NEG:NEG + EPG], t8, cmax)
            link(v.scalar_tensor_tensor(le_, oh1, -3e38, le_, ALU.mult, ALU.add))
            link(v.tensor_reduce(top2, le_, AX.X, ALU.max))
            first_of(oh2, le_, top2, EPG, ramp[:, NEG:NEG + EPG], t8, cmax)
            v.tensor_tensor(ev, top2, top1, ALU.subtract).then_inc(r_dve, 1)
            for out, oh in ((m1_, oh1), (m2_, oh2)):
                for a_ in range(NEG):
                    x = v.tensor_tensor(out[:, :, a_, :], oh, ohg[:, :, a_:a_ + 1].broadcast_to([P, TILES, EPG]), ALU.mult)
                link(x)
            fl = "p i a b -> p i (a b)"
            link(v.tensor_tensor(mm, m1_.rearrange(fl), m2_.rearrange(fl), ALU.add))
            link(v.tensor_copy(before[:, 0, :], mm[:, 0, :]))
            for i in range(1, TILES - 1):
                x = v.tensor_tensor(before[:, i, :], before[:, i - 1, :], mm[:, i, :], ALU.add)
                if i < TILES - 2:
                    link(x)
            x.then_inc(r_hot, 1)
            for n, m_ in enumerate((m1_, m2_)):
                link(v.tensor_tensor(tok_of[:, n * TILES:(n + 1) * TILES, :], m_.rearrange(fl), wide(tokid, NE), ALU.mult))
            dve.wait_ge(r_pos, 1)
            p3 = pr_.rearrange(fl)
            at2, (ec, fits, t_) = (sc[:, 8, :], sc[:, 12, :]), (sc[:, n, :] for n in (9, 10, 11))
            for n, m_ in enumerate((m1_, m2_)):
                at = at2[n]
                link(v.tensor_tensor(p3, m_.rearrange(fl), pO[:, 0:160].rearrange("p (i e) -> p i e", e=NE), ALU.mult))
                link(v.tensor_reduce(at, p3, AX.X, ALU.add))
                for i in range(TILES):
                    x = v.tensor_scalar(at_slot[:, n * TILES + i, :], places, at[:, i:i + 1], None, ALU.is_equal)
            x.then_inc(r_sel, 1)
            dve.wait_ge(r_idtr, 1)
            v.tensor_copy(ids[:, 0:NE], pS[0:CAP, 0:NE]).then_inc(r_ids, 1)
            dve.wait_ge(r_act, 2)
            link(v.tensor_reduce(gsum, t4, AX.X, ALU.add))
            link(v.reciprocal(gprob, gsum))
            link(v.tensor_scalar(v1s, ev, 1.0, None, ALU.add))
            link(v.reciprocal(v1s, v1s))
            link(v.tensor_tensor(gate[:, 0, :], v1s, gprob, ALU.mult))
            link(v.tensor_tensor(gate[:, 1, :], gate[:, 0, :], ev, ALU.mult))
            dve.wait_ge(r_pos, 2)
            link(v.tensor_reduce(cmax[0:1, 0:1], pY[0:1, 192:192 + NE], AX.X, ALU.max))
            for n, m_ in enumerate((m1_, m2_)):
                at = at2[n]
                link(v.tensor_tensor(p3, m_.rearrange(fl), eoff.unsqueeze(1).broadcast_to([P, TILES, NE]), ALU.mult))
                link(v.tensor_reduce(ec, p3, AX.X, ALU.add))
                link(v.scalar_tensor_tensor(t_, ec, float(1 + ROUNDS), at, ALU.mult, ALU.add))
                link(v.tensor_copy(slot_of[n], t_))
                link(v.tensor_scalar(fits, at, float(CAP), None, ALU.is_lt))
                link(v.tensor_tensor(t_, ec, at, ALU.add))
                link(v.tensor_tensor(t_, t_, fits, ALU.mult))
                link(v.tensor_copy(first_of_[n], t_))
                link(v.scalar_tensor_tensor(t_, ec, float(ROUNDS), at, ALU.mult, ALU.add))
                link(v.tensor_scalar(t_, t_, float(-CAP), None, ALU.add))
                link(v.tensor_tensor(gate_later[:, n, :], gate[:, n, :], fits, ALU.mult))
                link(v.tensor_tensor(ec, t_, fits, ALU.mult))
                link(v.tensor_tensor(t_, t_, ec, ALU.subtract))
                link(v.tensor_copy(later_of[n], t_))
                link(v.tensor_tensor(t_, gate[:, n, :], gate_later[:, n, :], ALU.subtract))
                link(v.tensor_copy(gate[:, n, :], gate_later[:, n, :]))
                link(v.tensor_copy(gate_later[:, n, :], t_))
            v.tensor_copy(most[0:1, 0:1], cmax[0:1, 0:1]).then_inc(r_slot, 1)
            with dve.Fori(0, NE // UNROLL) as t:
                for u in range(UNROLL):
                    e = t * UNROLL + u
                    dve.wait_ge(m_silu, e + 1)
                    b_ = pS if u % 2 else pT
                    v.tensor_tensor(gs[u % 2], gs[u % 2], b_[:, FK * CAP:2 * FK * CAP].rearrange("p (a b) -> p a b", a=FK),
                                    ALU.mult).then_inc(m_act, 1)
                    dve.wait_ge(e_done[u], t + 1)
                    dve.wait_ge(ye_out[u % 2], t * 32 + (16 * (u // 2) + 1))
                    if u % 2 == 0:
                        v.tensor_copy(ye[0][0:CAP, :], acc[1][0:CAP, :, :].rearrange("p a b -> p (a b)")).then_inc(m_ye, 1)
                    else:
                        v.tensor_copy(ye[1][0:CAP, 0:512], pY[0:CAP, :])
                        v.tensor_copy(ye[1][0:CAP, 512:1024], pO[0:CAP, :]).then_inc(m_ye, 1)
            dve.wait_ge(m_dn, NE)
            dve.wait_ge(ye_out[0], 16 * NE // 2 + 1)
            dve.wait_ge(ye_out[1], 16 * NE // 2 + 1)
            n_most = dve.value_load(most[0:1, 0:1], min_val=0, max_val=T)
            with dve.If(n_most > CAP):
                with dve.Fori(0, NE) as e:
                    with dve.Fori(0, ROUNDS) as r:
                        n = e * ROUNDS + r
                        dve.wait_ge(f_silu, n + 1)
                        v.tensor_tensor(gs[0], gs[0], pT[:, FK * CAP:2 * FK * CAP].rearrange("p (a b) -> p a b", a=FK),
                                        ALU.mult).then_inc(f_act, 1)
                        dve.wait_ge(f_dn, n + 1)
                        dve.wait_ge(f_out, n * 16 + 1)
                        v.tensor_copy(ye[0][0:CAP, :], acc[1][0:CAP, :, :].rearrange("p a b -> p (a b)")).then_inc(f_ye, 1)
                for i in range(TILES):
                    r = ROWS[i]
                    for n in range(2):
                        dve.wait_ge(f_back, 16 * (2 * i + n + 1))
                        v.scalar_tensor_tensor(x2[0:r, i, :], xe[0][0:r, :], gate_later[0:r, n, i:i + 1], x2[0:r, i, :],
                                               ALU.mult, ALU.add).then_inc(f_add, 1)
                        dve.wait_ge(f_add, 2 * i + n + 1)
            dve.sem_inc(f_skip, 1)
            def finish(i):
                r = ROWS[i]
                dve.wait_ge(z_sd, i + 1)
                link(v.reciprocal(stat[0:r, 2, i:i + 1], stat[0:r, 1, i:i + 1]))
                v.scalar_tensor_tensor(x2[0:r, i, :], x2[0:r, i, :], stat[0:r, 2, i:i + 1], fnb[0:r, :],
                                       ALU.mult, ALU.mult).then_inc(z_y, 1)

            for i in range(TILES):
                r = ROWS[i]
                dve.wait_ge(g_in[i], 32)
                for n in range(2):
                    x = v.scalar_tensor_tensor(x2[0:r, i, :], y_in[2 * i + n][0:r, :], gate[0:r, n, i:i + 1], x2[0:r, i, :],
                                               ALU.mult, ALU.add)
                    if n == 0:
                        link(x)
                x.then_inc(z_ss, 1)
                if i >= 1:
                    finish(i - 1)
            finish(TILES - 1)

        @block.scalar
        def _(act):
            a_ = nc.scalar
            act.sem_inc(s_exp, 1)
            act.sem_inc(s_silu, 2)
            act.sem_inc(hs_out, 1)
            act.sem_inc(so_out, 1)
            act.sem_inc(s_rm, 1)
            act.sem_inc(ye_out[0], 1)
            act.sem_inc(ye_out[1], 1)
            act.sem_inc(f_out, 1)
            for s in range(2):
                act.sem_inc(acc_free[s], 1)
            link = chain(act, act_chain, 0)

            def root(i, x, scratch, s_out):
                r = ROWS[i]
                link(a_.activation(scratch[0:r, :], x, ACT.Square, accum_out=stat[0:r, 0, i:i + 1]))
                a_.activation(stat[0:r, 1, i:i + 1], stat[0:r, 0, i:i + 1], ACT.Sqrt, bias=eps[0:r, :], scale=1.0 / D
                              ).then_inc(s_out, 1)

            act.wait_ge(consts, 1)
            for i in range(TILES):
                act.wait_ge(x_in[i], 32 if i in (0, 4) else 16)
                root(i, x_tok[0:ROWS[i], i, :], junk, s_sd)

            def split_hi(where, b, ahead=2):
                n, half, _, _ = where
                act.wait_ge(raw_in[b % 2], half * 16 + 8 * ahead + 16)
                a_.activation(w_hi[b % 2], w_raw[b % 2], ACT.Copy).then_inc(hi_done, 1)

            for b in range(2):
                split_hi(s_block(0, b), b, 0)
            for i in range(TILES):
                act.wait_ge(s_hT, i + 1)
                a_.activation(hT_hi[:, :, tok(i)], hT[:, :, tok(i)], ACT.Copy).then_inc(h_hi, 1)
            x_, ab, e_, u_, l_, z_ = (dtw[:, n, :] for n in range(6))
            act.wait_ge(s_dtv, 1)
            a_.activation(e_, ab, ACT.Exp, scale=-1.0).then_inc(s_dta, 1)
            act.wait_ge(s_dtv, 2)
            a_.activation(l_, u_, ACT.Ln).then_inc(s_dta, 1)
            a_.activation(ea, ea, ACT.Exp).then_inc(s_dta, 1)
            with act.Fori(0, 4) as t:
                for b in range(6):
                    use, _, a, ause = s_block(t, b)
                    act.wait_ge(w_done, use + 2)
                    split_hi(s_block(t, b), b)
                    if b % 3 == 0:
                        a0, a1 = acc_parts(acc[a])
                        c0, c1 = halves(s_c[:, b // 3, :])
                        a_.activation(c0, a0, ACT.Copy)
                        a_.activation(c1, a1, ACT.Copy).then_inc(acc_free[a], 1)
            act.wait_ge(s_cum, 1)
            f3 = "p (i h) -> p i h"
            a_.activation(e_acum[:, :, :], pY[:, 0:160].rearrange(f3, h=HEADS), ACT.Exp).then_inc(s_dta, 1)
            a_.activation(dte[:, :, :], pY[:, 160:320].rearrange(f3, h=HEADS), ACT.Exp).then_inc(s_dta, 1)
            a_.activation(dec[:, :, :], pY[:, 320:480].rearrange(f3, h=HEADS), ACT.Exp).then_inc(s_dta, 1)
            a_.activation(sdec[:, :], pS[0:R4, 0:HEADS], ACT.Exp).then_inc(s_dta, 1)
            s_so_buf = h0T[:, 0, :]
            def gate_of(where, j, read):
                _, _, a, ause = where
                act.wait_ge(o_m, read)
                a0, a1 = acc_parts(acc[a])
                g0, g1 = halves(sg[:, j, :])
                a_.activation(g0, a0, ACT.Sigmoid)
                a_.activation(g1, a1, ACT.Sigmoid).then_inc(acc_free[a], 1)
                act.wait_ge(acc_free[a], ause + 2)
                act.sem_inc(o_sg, 1)

            with act.Fori(0, 8) as f:
                for b in range(2):
                    use, _, a, ause = o1_block(f, b)
                    act.wait_ge(w_done, use + 2)
                    split_hi(o1_block(f, b), b)
                    if b == 0:
                        gate_of(o1_block(f, 0), 0, f + 1)
            act.wait_ge(w_done, g_block(0, 0)[0] + 2)
            split_hi(g_block(0, 0), 0)
            with act.Fori(0, GROUPS) as g:
                def silu(c):
                    act.wait_ge(s_cvd, g * 6 + (c + 3))
                    dst = cT if c == 0 else bT if c == 1 else xT[:, c - 2, :]
                    bias = xvec[:, bass.ds(conv_tile(g, c), 1), 4:5].rearrange("p a b -> p (a b)")
                    v0, v1_ = conv_parts(cv[:, c % 2, :], XH, XROW)
                    d0, d1 = halves(dst)
                    a_.activation(d0, v0, ACT.Silu, bias=bias)
                    a_.activation(d1.rearrange(seqs, c=SLEN), v1_, ACT.Silu, bias=bias).then_inc(s_silu, 1)

                def z_gate(k):
                    use, _, a, ause = g_block(g, 6 + k)
                    act.wait_ge(w_done, use + 2)
                    split_hi(g_block(g, 6 + k), k)
                    a0, a1 = acc_parts(acc[a])
                    d0, d1 = halves(sz[:, k, :])
                    a_.activation(d0, a0, ACT.Copy)
                    a_.activation(d1, a1, ACT.Copy).then_inc(acc_free[a], 1)

                for c in range(6):
                    use, _, a, ause = g_block(g, c)
                    act.wait_ge(w_done, use + 2)
                    if c >= 1:
                        split_hi(g_block(g, c), c)
                    act.wait_ge(s_tail, g * 6 + (c + 1))
                    act.wait_ge(s_cvd, g * 6 + (c + 1))
                    a0, a1 = acc_parts(acc[a])
                    d0, d1 = pad_parts(raw[:, c % 2, :], XH, XROW)
                    a_.activation(d0, a0, ACT.Copy)
                    a_.activation(d1, a1.rearrange(seqs, c=SLEN), ACT.Copy).then_inc(acc_free[a], 1)
                    for n in ((), (), (0, 1), (2,), (3,), (4,))[c]:
                        silu(n)
                silu(5)
                z_gate(0)
                for i in range(TILES):
                    r = ROWS[i]
                    act.wait_ge(p_cb, g * 5 + (i + 1))
                    a_.activation(btok[0:r, i % 2, :], pO[0:r, P:2 * P], ACT.Copy).then_inc(s_bt, 1)
                    act.wait_ge(p_y, g * 5 + (i + 1))
                    for q in range(2):
                        act.wait_ge(p_seg, g * 10 + (2 * i + q + 3))
                        a_.activation(wts[0:r, q, 0:4 * r], pS[0:r, 0:4 * r], ACT.Exp).then_inc(s_exp, 1)
                    if i < 3:
                        z_gate(i + 1)
                    if i == 4:
                        act.wait_ge(so_out, g * 16 + 1)
                        for b in range(NSEQ):
                            act.wait_ge(p_h0, g * 8 + (b + 1))
                            act.wait_ge(p_yb, g * 8 + (b + 1))
                            a_.activation(h0T[:, b % 2, :], acc[b % 4 // 2][:, b % 2, :], ACT.Copy).then_inc(s_h0, 1)
                act.wait_ge(acc_free[1], g * 5 + 26)
                act.wait_ge(acc_free[0], g * 5 + 26)
                a_.activation(sz, sz, ACT.Silu).then_inc(s_sz, 1)
                act.wait_ge(p_so, g + 1)
                a_.activation(s_so_buf, pT[:, :], ACT.Copy).then_inc(s_so, 1)
                act.wait_ge(s_so, g + 1)
                dst = outs[2][0, 0].rearrange("h p n -> (h p) n")[bass.ds(g * GW, GW), :]
                act.dma_start(dst.rearrange("(k p) n -> p k n", p=P), s_so_buf.rearrange("p (k n) -> p k n", k=GK)
                              ).then_inc(so_out, 16)
                act.wait_ge(s_uz, g + 1)
                u_g = uT[:, bass.ds(g * GK, GK), :]
                a_.activation(sq, u_g, ACT.Square).then_inc(s_sq, 1)
                act.wait_ge(w_done, g_block(g, 10)[0] + 2)
                split_hi(g_block(g, 10), 10)
                act.wait_ge(p_gn, g + 1)
                a_.activation(rms[:, 0:HALF], pT[:, 0:HALF], ACT.Sqrt, bias=eps[:, :], scale=1.0 / GW)
                a_.activation(rms[:, HALF:T], pS[:, 0:T - HALF], ACT.Sqrt, bias=eps[:, :], scale=1.0 / GW).then_inc(s_rm, 1)
            act.wait_ge(s_tail, GROUPS * 6 + 2)
            for c in range(4):
                act.wait_ge(s_un, c + 1)
                a_.activation(uT_hi[:, 4 * c:4 * c + 4, :], uT[:, 4 * c:4 * c + 4, :], ACT.Copy).then_inc(u_hi, 1)
                if c == 1:
                    gate_of(o2_block(0, 0), 0, 8)

            def mixer_turn(t, last):
                for b in range(1, 4 if last else 7):
                    act.wait_ge(w_done, o2_block(t, b)[0] + 2)
                    split_hi(o2_block(t, b), b)
                    if b == 1:
                        gate_of(o2_block(t, 1), 1, t * 2 + 9)
                    if b == 6:
                        gate_of(o2_block(t, 6), 0, t * 2 + 10)

            with act.Fori(0, 3) as t:
                mixer_turn(t, False)
            act.wait_ge(hs_out, 64 * GROUPS + 1)
            act.wait_ge(so_out, 16 * GROUPS + 1)
            act.dma_start(wo[0], cols(ins["w_o"][0], 0, 512)).then_inc(wo_in[0], 16)
            mixer_turn(3, True)
            for i in range(TILES):
                act.wait_ge(r_x2, TILES + i + 1)
                if i >= 1:
                    act.wait_ge(r_sd, i)
                root(i, x2[0:ROWS[i], i, :], sqj, r_sd)
                act.wait_ge(r_h2, i + 1)
                act.dma_start(h2_rows[tok(i), :], h2[0:ROWS[i], i % 2, :]).then_inc(h2_out[i % 2], 16)
            act.wait_ge(r_dve, 1)
            a_.activation(t4, t4, ACT.Exp).then_inc(r_act, 1)
            act.wait_ge(r_dve, 2)
            a_.activation(sc[:, 5, :], sc[:, 5, :], ACT.Exp).then_inc(r_act, 1)
            act.wait_ge(r_act, 2)
            banks = [acc[0][:, 0, :], acc[0][:, 1, :], acc[1][:, 0, :], acc[1][:, 1, :]]
            for n in range(8):
                act.wait_ge(p_tl, n + 1)
                rr = TAIL if n < 6 else STAIL
                a_.activation(tails[0:rr, n * 512:(n + 1) * 512], banks[n % 4][0:rr, :], ACT.Copy).then_inc(s_tl, 1)
            act.wait_ge(s_tl, 8)
            act.dma_start(outs[3][0, 0], tails[0:XH, 0:CONV]).then_inc(tails_out, 16)
            act.dma_start(outs[6][0].rearrange("b r c -> (b r) c"), tails[XH:TAIL, 0:CONV]).then_inc(tails_out, 16)
            act.dma_start(outs[4][0, 0], tails[0:SH, CONV:]).then_inc(tails_out, 16)
            act.dma_start(outs[7][0].rearrange("b r c -> (b r) c"), tails[SH:STAIL, CONV:]).then_inc(tails_out, 16)
            act.wait_ge(m_tr, 1)
            a_.activation(xeT[0].rearrange("p (a k) c -> p a (k c)", a=2), acc[0][:, :, 0:4 * CAP], ACT.Copy).then_inc(m_xe, 1)
            with act.Fori(0, NE // UNROLL) as t:
                for u in range(UNROLL):
                    e = t * UNROLL + u
                    act.wait_ge(m_gu, e + 1)
                    b_ = pS if u % 2 else pT
                    a_.activation(gs[u % 2], b_[:, 0:FK * CAP].rearrange("p (a b) -> p a b", a=FK), ACT.Silu).then_inc(m_silu, 1)
                    act.wait_ge(m_tr, e + 2)
                    a_.activation(xeT[(u + 1) % 2].rearrange("p (a k) c -> p a (k c)", a=2), acc[0][:, :, 0:4 * CAP], ACT.Copy
                                  ).then_inc(m_xe, 1)
                    act.wait_ge(m_ye, e + 2)
                    act.dma_start(y_first[bass.ds(e * CAP, CAP), :], ye[u % 2][0:CAP, :]).then_inc(ye_out[u % 2], 16)
            act.wait_ge(m_dn, NE)
            n_most = act.value_load(most[0:1, 0:1], min_val=0, max_val=T)
            with act.If(n_most > CAP):
                with act.Fori(0, NE) as e:
                    with act.Fori(0, ROUNDS) as r:
                        n = e * ROUNDS + r
                        act.wait_ge(f_tr, n + 1)
                        a_.activation(xeT[0].rearrange("p (a k) c -> p a (k c)", a=2), acc[0][:, :, 0:4 * CAP], ACT.Copy
                                      ).then_inc(f_xe, 1)
                        act.wait_ge(f_gu, n + 1)
                        a_.activation(gs[0], pT[:, 0:FK * CAP].rearrange("p (a b) -> p a b", a=FK), ACT.Silu).then_inc(f_silu, 1)
                        act.wait_ge(f_ye, n + 1)
                        act.dma_start(y_later[bass.ds(n * CAP, CAP), :], ye[0][0:CAP, :]).then_inc(f_out, 16)
                        act.wait_ge(f_out, n * 16 + 17)
            for i in range(TILES):
                act.wait_ge(z_ss, i + 1)
                root(i, x2[0:ROWS[i], i, :], sqj, z_sd)

        @block.gpsimd
        def _(pool):
            held[id(pool)] = sem("held_pool")
            gp = nc.gpsimd
            link = chain(pool, pool_chain, 0)
            pool.sem_inc(c_tail, 2)
            pool.sem_inc(lo_done, 2)
            pool.sem_inc(s_tail, 2)
            for m in (ones, m_le, m_gt, m_blk4):
                gp.memset(m[:, :], 1.0)
            gp.memset(eps[:, :], EPS)
            link(gp.memset(ident[:, :], 0.0))

            def select(out, in_, pattern, base, mult, op=ALU.is_ge, fill=0.0):
                link(gp.affine_select(out=out, in_=in_, pattern=pattern, compare_op=op, fill=fill, base=base,
                                      channel_multiplier=mult))

            select(ident[:, :], ident[:, :], [[-1, P]], 0, 1, ALU.not_equal, 1.0)
            select(m_le[:, :], m_le[:, :], [[1, P]], 0, -1)
            select(m_gt[:, :], m_gt[:, :], [[-1, P]], -1, 1)
            blk = m_blk4[:, 0:LASTP]
            select(blk, blk, [[0, LASTP]], LASTP - 1, -1)
            blk = m_blk4[:, LASTP:R4].rearrange("p (s c) -> p s c", c=SLEN)
            select(blk, blk, [[-SLEN, NSEQ], [0, SLEN]], -LASTP, 1)
            select(blk, blk, [[SLEN, NSEQ], [0, SLEN]], LASTP + SLEN - 1, -1)
            select(m_le4[:, :], m_blk4[:, :], [[1, R4]], 0, -1)
            gp.affine_select(out=m_gt4[:, :], in_=m_blk4[:, :], pattern=[[-1, R4]], compare_op=ALU.is_ge, fill=0.0,
                             base=-1, channel_multiplier=1).then_inc(consts, 1)

            def split_lo(where, b, ahead=2):
                pool.wait_ge(hi_done, where[0] + (ahead + 1))
                gp.tensor_tensor(w_lo[b % 2], w_raw[b % 2], w_hi[b % 2].bitcast(F32), ALU.subtract).then_inc(lo_done, 1)

            for b in range(2):
                split_lo(s_block(0, b), b, 0)
            for i in range(TILES):
                pool.wait_ge(h_hi, i + 1)
                gp.tensor_tensor(hT_lo[:, :, tok(i)], hT[:, :, tok(i)], hT_hi[:, :, tok(i)].bitcast(F32), ALU.subtract
                                 ).then_inc(h_lo, 1)
            pool.wait_ge(s_vcp, 4)
            link(gp.memset(s_pad[:, 0, 0:SH], 0.0))
            link(gp.memset(s_pad[:, 1, 0:SH], 0.0))
            start = link.count[0]
            with pool.Fori(0, 4) as t:
                for j in range(2):
                    hold(pool, c_conv, t * 2 + (j + 1))
                    f = bass.ds(t * 2 + j, 1)
                    rows = s_pad[:, j, SH + TP:SH + TP + NSEQ * SROW].rearrange("p (s c) -> p s c", c=SROW)
                    h_f = svec[:, f, 3:19].rearrange("p a (s c) -> p (a s) c", c=SH)
                    gp.tensor_copy(rows[:, :, 0:SH], h_f).then_inc(c_hist, 1)
                for j in range(2):
                    split_lo(s_block(t, 3 * j), 3 * j)
                    split_lo(s_block(t, 3 * j + 1), 3 * j + 1)
                    f = bass.ds(t * 2 + j, 1)
                    _, _, a, ause = s_block(t, 3 * j + 1)
                    hold(pool, acc_free[a], ause + 2)
                    rows = s_pad[:, j, SH + TP:SH + TP + NSEQ * SROW].rearrange("p (s c) -> p s c", c=SROW)
                    gp.tensor_copy(stail[:, f, 0:SH].rearrange("p a b -> p (a b)"), s_pad[:, j, TP:TP + SH])
                    gp.tensor_copy(stail[:, f, SH:STAIL].rearrange("p a (s c) -> p (a s) c", c=SH), rows[:, :, SLEN:SROW]
                                   ).then_inc(c_tail, 1)
                    split_lo(s_block(t, 3 * j + 2), 3 * j + 2)
                hold(pool, c_conv, t * 2 + 4)
            with pool.Fori(0, 8) as f:
                for b in range(2):
                    split_lo(o1_block(f, b), b)
            pool.wait_ge(acc_free[1], 13)
            pool.wait_ge(acc_free[0], 13)
            link = chain(pool, pool_chain, start)
            link(gp.memset(raw[:, 0, 0:XH], 0.0))
            link(gp.memset(raw[:, 1, 0:XH], 0.0))
            link(gp.memset(cmask, 0.0))
            split_lo(g_block(0, 0), 0)
            with pool.Fori(0, GROUPS) as g:
                def history(c):
                    hold(pool, s_cvd, g * 6 + (c + 1))
                    f = bass.ds(conv_tile(g, c), 1)
                    rows = raw[:, c % 2, XH + TP:XPAD].rearrange("p (s c) -> p s c", c=XROW)
                    gp.tensor_copy(rows[:, :, 0:XH], xvec[:, f, 5:29].rearrange("p a (s c) -> p (a s) c", c=XH)
                                   ).then_inc(s_hist, 1)

                def tail(c):
                    _, _, a, ause = g_block(g, c)
                    hold(pool, acc_free[a], ause + 2)
                    f = bass.ds(conv_tile(g, c), 1)
                    rows = raw[:, c % 2, XH + TP:XPAD].rearrange("p (s c) -> p s c", c=XROW)
                    gp.tensor_copy(xtail[:, f, 0:XH].rearrange("p a b -> p (a b)"), raw[:, c % 2, TP:TP + XH])
                    gp.tensor_copy(xtail[:, f, XH:TAIL].rearrange("p a (s c) -> p (a s) c", c=XH), rows[:, :, SLEN:XROW]
                                   ).then_inc(s_tail, 1)

                history(0)
                history(1)
                for c in range(6):
                    if c >= 1:
                        split_lo(g_block(g, c), c)
                        if c < 5:
                            history(c + 1)
                    tail(c)

                def decays(i, q):
                    r = ROWS[i]
                    le = m_le if i < 4 else m_le4
                    hold(pool, p_seg, g * 10 + (2 * i + q + 1))
                    gp.tensor_tensor(rbuf[0:r, q, 0:4 * r].rearrange("p (h c) -> p h c", h=4),
                                     le[0:r, 0:r].unsqueeze(1).broadcast_to([r, 4, r]),
                                     da[0:r, i, bass.ds(g * HPG + 4 * q, 4)].unsqueeze(2).broadcast_to([r, 4, r]),
                                     ALU.mult).then_inc(s_r, 1)

                decays(0, 0)
                decays(0, 1)
                split_lo(g_block(g, 6), 6)
                for i in range(1, TILES):
                    for q in range(2):
                        decays(i, q)
                    if i < 4:
                        split_lo(g_block(g, 6 + i), 6 + i)
                    if i == 1:
                        hold(pool, s_silu, g * 6 + 8)
                        gp.tensor_copy(cmask[:, 0:LASTP], cT[:, 4 * P:TP])
                        diag = cmask[:, R4 + LASTP:R4 + LASTP + NSEQ * (R4 + SLEN)].rearrange("p (s c) -> p s c", c=R4 + SLEN)
                        gp.tensor_copy(diag[:, :, 0:SLEN], cT[:, TP:T].rearrange("p (s c) -> p s c", c=SLEN)).then_inc(s_cm, 1)
                hold(pool, s_bt, g * 5 + 5)
                hold(pool, p_seg, g * 10 + 12)
                gp.tensor_tensor(bmask[0:R4], btok[0:R4, 0, :].unsqueeze(1).broadcast_to([R4, NSEQ, NST]),
                                 m_blk4[:, LASTP:R4:SLEN].unsqueeze(2).broadcast_to([R4, NSEQ, NST]), ALU.mult
                                 ).then_inc(s_bm, 1)
                hold(pool, s_df, g + 1)
                hold(pool, p_h0, g * 8 + 8)
                for k in range(GK):
                    gp.tensor_tensor(hs[:, k], hs[:, k], df[:, k, :].unsqueeze(2).broadcast_to([P, NSEQ, NST]), ALU.mult
                                     ).then_inc(s_hd, 1)
                hold(pool, p_yb, g * 8 + 10)
                hold(pool, p_hs, g * 4 + 4)
                split_lo(g_block(g, 10), 10)
            pool.wait_ge(u_hi, 1)
            gp.tensor_tensor(uT_lo[:, 0:4, :], uT[:, 0:4, :], uT_hi[:, 0:4, :].bitcast(F32), ALU.subtract).then_inc(h_lo, 1)
            def mixer_turn(t, last):
                for b in range(1, 4 if last else 7):
                    split_lo(o2_block(t, b), b)

            with pool.Fori(0, 3) as t:
                mixer_turn(t, False)
            mixer_turn(3, True)
            pool.wait_ge(w_done, BLOCKS + 1)
            pool.wait_ge(o_m, 17)
            link(gp.memset(m_lt, 1.0))
            select(m_lt, m_lt, [[1, P]], -1, -1)
            gp.memset(zero, 0.0)
            gp.memset(ids[:, :], 0)
            gp.iota(ramp[:, 0:NEG], pattern=[[-1, NEG]], base=NEG, channel_multiplier=0, allow_small_or_imprecise_dtypes=True)
            gp.iota(ramp[:, NEG:NEG + EPG], pattern=[[-1, EPG]], base=EPG, channel_multiplier=0,
                    allow_small_or_imprecise_dtypes=True)
            gp.iota(places, pattern=[[1, CAP]], base=0, channel_multiplier=0, allow_small_or_imprecise_dtypes=True)
            gp.iota(eoff, pattern=[[CAP, NE]], base=0, channel_multiplier=0, allow_small_or_imprecise_dtypes=True)
            gp.iota(tokid, pattern=[[P, TILES]], base=0, channel_multiplier=1, allow_small_or_imprecise_dtypes=True
                    ).then_inc(r_const, 1)
            pool.wait_ge(r_ids, 1)
            pool.wait_ge(h2_out[0], 48)
            pool.wait_ge(h2_out[1], 32)

            def gather(u, index):
                pool.indirect_dma_start(xe[u][0:CAP, :], None, h2_rows[:, :],
                                        bass.IndirectOffsetOnAxis(ap=index[0:CAP, 0:1], axis=0)).then_inc(xe_in[u], 16)

            gp.tensor_copy(idx[0][:, :], ids[:, 0:1]).then_inc(m_idx, 1)
            pool.wait_ge(m_idx, 1)
            gather(0, idx[0])
            with pool.Fori(0, NE // UNROLL) as t:
                for u in range(UNROLL):
                    e = t * UNROLL + u
                    un = (u + 1) % UNROLL
                    hold(pool, m_tr, e + 1)
                    gp.tensor_copy(idx[un][:, :], ids[:, bass.ds(e + 1, 1)]).then_inc(m_idx, 1)
                    hold(pool, m_idx, e + 2)
                    gather(un, idx[un])
            pool.wait_ge(m_dn, NE)
            n_most = pool.value_load(most[0:1, 0:1], min_val=0, max_val=T)
            with pool.If(n_most > CAP):
                pool.wait_ge(id_zero, 16)
                for i in range(TILES):
                    for n in range(2):
                        pool.indirect_dma_start(id_tab[:, :], bass.IndirectOffsetOnAxis(ap=slot_of[n][0:ROWS[i], i:i + 1], axis=0),
                                                tokid[0:ROWS[i], i:i + 1], None).then_inc(r_tab, 16)
                with pool.Fori(0, NE) as e:
                    with pool.Fori(0, ROUNDS) as r:
                        n = e * ROUNDS + r
                        hold(pool, f_id, n * 16 + 16)
                        gp.tensor_copy(idx[0][:, :], idf[:, :]).then_inc(f_cast, 1)
                        hold(pool, f_cast, n + 1)
                        pool.indirect_dma_start(xe[0][0:CAP, :], None, h2_rows[:, :],
                                                bass.IndirectOffsetOnAxis(ap=idx[0][0:CAP, 0:1], axis=0)).then_inc(f_x, 16)
                        hold(pool, f_x, n * 16 + 16)
                pool.wait_ge(f_out, 16 * NE * ROUNDS + 1)
                for i in range(TILES):
                    for n in range(2):
                        if 2 * i + n:
                            pool.wait_ge(f_add, 2 * i + n)
                        pool.indirect_dma_start(xe[0][0:ROWS[i], :], None, y_later[:, :],
                                                bass.IndirectOffsetOnAxis(ap=later_of[n][0:ROWS[i], i:i + 1], axis=0)
                                                ).then_inc(f_back, 16)
            pool.wait_ge(ye_out[0], 16 * NE // 2 + 1)
            pool.wait_ge(ye_out[1], 16 * NE // 2 + 1)
            pool.wait_ge(f_skip, 1)
            for i in range(TILES):
                for n in range(2):
                    pool.indirect_dma_start(y_in[2 * i + n][0:ROWS[i], :], None, y_first[:, :],
                                            bass.IndirectOffsetOnAxis(ap=first_of_[n][0:ROWS[i], i:i + 1], axis=0)
                                            ).then_inc(g_in[i], 16)


NAMES = ["x_prompt", "x_sample", "state_ssm", "state_ssd_conv", "state_short_conv", "meta_tokens", "ln1_w", "w_in",
         "ssd_conv_w", "ssd_conv_b", "ssd_dt_bias", "ssd_A_log", "ssd_D", "ssd_norm_w", "w_ssd_out", "sc_conv_w",
         "w_sc_out", "w_o", "ln2_w", "w_rg", "b_rg", "w_re", "b_re", "w_gate", "w_up", "w_down", "final_norm_w"]
OUTS = [(1, SEQ, D), (NSEQ, SLEN, D), (1, 1, HEADS, HD, NST), (1, 1, XH, CONV), (1, 1, SH, D),
        (1, NSEQ, HEADS, HD, NST), (1, NSEQ, XH, CONV), (1, NSEQ, SH, D)]


def kernel(**inputs):
    import numpy as np
    import concourse.bacc as bacc
    from concourse.bass_utils import run_bass_kernel_spmd
    nc = bacc.Bacc("TRN2", target_bir_lowering=False, num_devices=1)
    arrays, ins, outs = {}, {}, []
    for n in NAMES:
        a = np.ascontiguousarray(inputs[n])
        arrays["in_" + n] = a
        ins[n] = nc.dram_tensor("in_" + n, a.shape, mybir.dt.from_np(a.dtype), kind="ExternalInput").ap()
    for i, s in enumerate(OUTS):
        outs.append(nc.dram_tensor(f"out_{i}", s, F32, kind="ExternalOutput").ap())
    build(nc, ins, outs)
    r = run_bass_kernel_spmd(nc, [arrays], core_ids=[0])
    return tuple(r.results[0][f"out_{i}"] for i in range(len(OUTS)))
```
